# Optimizing a Trainium2 kernel written in Bass

```python
import math
import jax, jax.numpy as jnp
from jax import lax
import numpy as np

D_MODEL = 1024
BATCH = 1
SEQ = 2048
DEPTH = 1

CHUNK = 64
WINDOW = 128
WIN_CHUNKS = WINDOW // CHUNK

A_HEADS = 8
A_KV_HEADS = 2
A_HEAD_DIM = 64
A_GROUP = A_HEADS // A_KV_HEADS
A_WIDTH = A_HEADS * A_HEAD_DIM
A_KV_WIDTH = A_KV_HEADS * A_HEAD_DIM

B_HEADS = 4
B_KEY_DIM = 64
B_VAL_DIM = 128
B_QK_WIDTH = B_HEADS * B_KEY_DIM
B_WIDTH = B_HEADS * B_VAL_DIM
B_GATE_RANK = 16
B_GATE_NORM = 16.0

N_BRANCHES = 2
RMS_EPS = 1e-6
NEG_INF = -1e30

SPLIT_SIZES = (A_WIDTH, A_KV_WIDTH, A_KV_WIDTH, A_WIDTH,
               B_QK_WIDTH, B_QK_WIDTH, B_WIDTH, B_WIDTH,
               B_GATE_RANK, N_BRANCHES * D_MODEL)
D_IN = (A_WIDTH + 2 * A_KV_WIDTH + A_WIDTH + 2 * B_QK_WIDTH + 2 * B_WIDTH
        + B_GATE_RANK + N_BRANCHES * D_MODEL)

kernel_name = "hybrid_swa_sink_gla_adaln"

def rms_norm(x, g):
    xf = x.astype(jnp.float32)
    y = xf * lax.rsqrt(jnp.mean(xf * xf, axis=-1, keepdims=True) + RMS_EPS)
    return (y * g.astype(jnp.float32)).astype(x.dtype)

def split_columns(proj):
    offsets = []
    acc = 0
    for s in SPLIT_SIZES[:-1]:
        acc += s
        offsets.append(acc)
    return jnp.split(proj, offsets, axis=-1)

def alibi_slopes(n_heads):
    return jnp.exp2(-8.0 * jnp.arange(1, n_heads + 1, dtype=jnp.float32) / n_heads)

def swa_sink_attention(q, k, v, sinks):
    b, s = q.shape[0], q.shape[1]
    nc = s // CHUNK
    pad = (WIN_CHUNKS - 1) * CHUNK
    qc = q.reshape(b, nc, CHUNK, A_KV_HEADS, A_GROUP, A_HEAD_DIM)
    kp = jnp.pad(k, ((0, 0), (pad, 0), (0, 0), (0, 0))).reshape(b, nc + WIN_CHUNKS - 1, CHUNK, A_KV_HEADS, A_HEAD_DIM)
    vp = jnp.pad(v, ((0, 0), (pad, 0), (0, 0), (0, 0))).reshape(b, nc + WIN_CHUNKS - 1, CHUNK, A_KV_HEADS, A_HEAD_DIM)
    kwin = jnp.concatenate([kp[:, w:w + nc] for w in range(WIN_CHUNKS)], axis=2)
    vwin = jnp.concatenate([vp[:, w:w + nc] for w in range(WIN_CHUNKS)], axis=2)
    scale = 1.0 / math.sqrt(A_HEAD_DIM)
    scores = jnp.einsum('bcqhgd,bcshd->bchgqs', qc, kwin).astype(jnp.float32) * scale
    q_pos = jnp.arange(CHUNK, dtype=jnp.float32) + pad
    k_pos = jnp.arange(WINDOW, dtype=jnp.float32)
    dist = jnp.abs(q_pos[:, None] - k_pos[None, :])
    slopes = alibi_slopes(A_HEADS).reshape(A_KV_HEADS, A_GROUP)
    scores = scores - slopes[:, :, None, None] * dist
    key_chunk = (jnp.arange(nc)[:, None] - (WIN_CHUNKS - 1)
                 + (jnp.arange(WINDOW) // CHUNK)[None, :])
    valid = (key_chunk >= 0)[None, :, None, None, None, :]
    scores = jnp.where(valid, scores, NEG_INF)
    sink = jnp.broadcast_to(sinks.astype(jnp.float32).reshape(1, 1, A_KV_HEADS, A_GROUP, 1, 1),
                            scores.shape[:-1] + (1,))
    probs = jax.nn.softmax(jnp.concatenate([scores, sink], axis=-1), axis=-1)[..., :-1]
    out = jnp.einsum('bchgqs,bcshd->bcqhgd', probs.astype(v.dtype), vwin)
    return out.reshape(b, s, A_WIDTH)

def gla_chunk_causal(q, k, v, log_alpha):
    b, s = q.shape[0], q.shape[1]
    nc = s // CHUNK
    qc = q.reshape(b, nc, CHUNK, B_HEADS, B_KEY_DIM).astype(jnp.float32) * (B_KEY_DIM ** -0.5)
    kc = k.reshape(b, nc, CHUNK, B_HEADS, B_KEY_DIM).astype(jnp.float32)
    vc = v.reshape(b, nc, CHUNK, B_HEADS, B_VAL_DIM).astype(jnp.float32)
    la = log_alpha.reshape(b, nc, CHUNK, B_HEADS, B_KEY_DIM)
    cum = jnp.cumsum(la, axis=2)
    total = cum[:, :, -1]
    k_dec = kc * jnp.exp(total[:, :, None] - cum)
    kv = jnp.einsum('bcshk,bcshv->bchkv', k_dec, vc)
    decay = jnp.exp(total)

    def step(state, inp):
        d, u = inp
        state = d[..., None] * state + u
        return state, state

    init = jnp.zeros((b, B_HEADS, B_KEY_DIM, B_VAL_DIM), jnp.float32)
    _, states = lax.scan(step, init, (jnp.moveaxis(decay, 1, 0), jnp.moveaxis(kv, 1, 0)))
    states = jnp.moveaxis(states, 0, 1)
    o = jnp.einsum('bcqhk,bchkv->bcqhv', qc, states)
    return o.reshape(b, s, B_HEADS, B_VAL_DIM).astype(q.dtype)

def hybrid_layer(x, mod, g_norm, w_in, w_alpha, b_alpha, sinks, g_head, w_br_a, w_br_b, w_out):
    b, s, _ = x.shape
    shift, scale, gate = jnp.split(mod, 3, axis=-1)
    h = rms_norm(x, g_norm) * (1.0 + scale[:, None, :]) + shift[:, None, :]
    proj = h @ w_in
    qa, ka, va, ga, qb, kb, vb, gb, za, zm = split_columns(proj)

    ya = swa_sink_attention(qa.reshape(b, s, A_HEADS, A_HEAD_DIM),
                            ka.reshape(b, s, A_KV_HEADS, A_HEAD_DIM),
                            va.reshape(b, s, A_KV_HEADS, A_HEAD_DIM), sinks)
    ya = ya * jax.nn.silu(ga)

    log_alpha = jax.nn.log_sigmoid((za @ w_alpha + b_alpha).astype(jnp.float32)) / B_GATE_NORM
    ob = gla_chunk_causal(qb.reshape(b, s, B_HEADS, B_KEY_DIM),
                          kb.reshape(b, s, B_HEADS, B_KEY_DIM),
                          vb.reshape(b, s, B_HEADS, B_VAL_DIM),
                          log_alpha.reshape(b, s, B_HEADS, B_KEY_DIM))
    yb = rms_norm(ob, g_head).reshape(b, s, B_WIDTH) * jax.nn.silu(gb)

    merge = jax.nn.sigmoid(zm).reshape(b, s, N_BRANCHES, D_MODEL)
    merged = merge[:, :, 0, :] * (ya @ w_br_a) + merge[:, :, 1, :] * (yb @ w_br_b)
    out = merged @ w_out
    return x + gate[:, None, :] * out

def setup_inputs(seed: int = 0) -> dict:
    key = jax.random.key(seed)
    ks = jax.random.split(key, 14)
    f32 = jnp.float32
    x = jax.random.normal(ks[0], (BATCH, SEQ, D_MODEL), f32)
    c = jax.random.normal(ks[1], (BATCH, D_MODEL), f32)
    ada_w = jax.random.normal(ks[2], (DEPTH, D_MODEL, 3 * D_MODEL), f32) * (0.5 * D_MODEL ** -0.5)
    ada_b = jax.random.normal(ks[3], (DEPTH, 3 * D_MODEL), f32) * 0.02
    norm_g = 1.0 + 0.02 * jax.random.normal(ks[4], (DEPTH, D_MODEL), f32)
    w_in = jax.random.normal(ks[5], (DEPTH, D_MODEL, D_IN), f32) * (D_MODEL ** -0.5)
    w_alpha = jax.random.normal(ks[6], (DEPTH, B_GATE_RANK, B_QK_WIDTH), f32) * (B_GATE_RANK ** -0.5)
    b_alpha = jax.random.normal(ks[7], (DEPTH, B_QK_WIDTH), f32) * 0.1
    sinks = jax.random.normal(ks[8], (DEPTH, A_HEADS), f32) * 0.5
    head_norm_g = 1.0 + 0.02 * jax.random.normal(ks[9], (DEPTH, B_VAL_DIM), f32)
    w_branch_a = jax.random.normal(ks[10], (DEPTH, A_WIDTH, D_MODEL), f32) * (A_WIDTH ** -0.5)
    w_branch_b = jax.random.normal(ks[11], (DEPTH, B_WIDTH, D_MODEL), f32) * (B_WIDTH ** -0.5)
    w_out = jax.random.normal(ks[12], (DEPTH, D_MODEL, D_MODEL), f32) * (D_MODEL ** -0.5)
    final_norm_g = 1.0 + 0.02 * jax.random.normal(ks[13], (D_MODEL,), f32)
    return {"x": x, "c": c, "ada_w": ada_w, "ada_b": ada_b, "norm_g": norm_g,
            "w_in": w_in, "w_alpha": w_alpha, "b_alpha": b_alpha, "sinks": sinks,
            "head_norm_g": head_norm_g, "w_branch_a": w_branch_a, "w_branch_b": w_branch_b,
            "w_out": w_out, "final_norm_g": final_norm_g}

def reference(x, c, ada_w, ada_b, norm_g, w_in, w_alpha, b_alpha, sinks, head_norm_g,
              w_branch_a, w_branch_b, w_out, final_norm_g):
    c_act = jax.nn.silu(c)
    for l in range(DEPTH):
        mod = c_act @ ada_w[l] + ada_b[l]
        x = hybrid_layer(x, mod, norm_g[l], w_in[l], w_alpha[l], b_alpha[l], sinks[l],
                         head_norm_g[l], w_branch_a[l], w_branch_b[l], w_out[l])
    return rms_norm(x, final_norm_g)


_drawn_inputs = setup_inputs


def setup_inputs(seed=0):
    import zlib

    import numpy as np

    out = dict(_drawn_inputs(seed))
    spreads = {}
    factors = {'ada_b': 5.238,
     'norm_g': 8.0,
     'b_alpha': 8.0,
     'sinks': 8.0,
     'head_norm_g': 29.23,
     'final_norm_g': 7.645}
    for name, (base, spread) in spreads.items():
        noise = np.random.default_rng([zlib.crc32(name.encode()), seed]).standard_normal(out[name].shape)
        drawn = base * np.exp(spread * noise) if base else spread * noise
        out[name] = __import__('jax').numpy.asarray(drawn.astype(out[name].dtype))
    for name, factor in factors.items():
        out[name] = (out[name] * factor).astype(out[name].dtype)
    return out
```

```python
import numpy as np
import concourse.bass as bass
from concourse import mybir

P = 128
D = 1024
SEQ = 2048
NT = 512
TILES = SEQ // NT
KB_D = D // P
TB = NT // P
CHUNK = 64
A_HEADS, A_GROUP, A_DIM = 8, 4, 64
WIN = 3 * CHUNK
B_HEADS, B_K, B_V = 4, 64, 128
RANK = 16
EPS = 1e-6
MASKED = 1e33
SINK_SCALE = 8.0
RSQRT_MAGIC = 0x5F3759DF

QA, KA, VA, GA, QB, KB, VB, GB, ZA, ZM = 0, 512, 640, 768, 1280, 1536, 1792, 2304, 2816, 2832
PANELS = [
    ("w_in", [(QA, 512)]),
    ("w_in", [(KA, 256), (QB, 256)]),
    ("w_in", [(GA, 512)]),
    ("w_in", [(KB, 256), (ZA, RANK)]),
    ("w_in", [(VB, 512)]),
    ("w_in", [(GB, 512)]),
    ("w_in", [(ZM, 512)]),
    ("w_in", [(ZM + D, 512)]),
    ("w_br", [(0, 512)]),
    ("w_in", [(ZM + 512, 512)]),
    ("w_in", [(ZM + D + 512, 512)]),
    ("w_br", [(512, 512)]),
    ("w_out", [(0, 512)]),
    ("w_out", [(512, 512)]),
]
P_QA, P_KVQ, P_GA, P_KZ, P_VB, P_GB = range(6)
P_ZM = (6, 7, 9, 10)
P_BR = (8, 11)
P_OUT = (12, 13)
SLOTS = 4 * len(PANELS)
DUOS = 4 * len(PANELS)
RING = 7
STAGES = 2
WIDTH = [sum(n for _, n in cols) for _, cols in PANELS]
FILLS = SLOTS + 8


def first_fill(slot):
    return slot + sum(min(max(slot - 4 * p, 0), 4) for p in P_BR)


def build(nc, x, c, ada_w, ada_b, norm_g, w_in, w_alpha, b_alpha, sinks, head_g, w_br_a, w_br_b, w_out,
          final_g, ada_b_row, ident_in, suffix_in, chunks_in, dist_in, out):
    F32, F32R, I32 = mybir.dt.float32, mybir.dt.float32r, mybir.dt.int32
    ACT, ALU, AX = mybir.ActivationFunctionType, mybir.AluOpType, mybir.AxisListType
    KIB = 1024

    cursor = [(nc.sbuf_base + 63) // 64 * 64]

    def place(name, shape, dt=F32, at=None):
        size = 4 * int(np.prod(shape[1:]))
        offset = cursor[0] if at is None else at
        if at is None:
            cursor[0] += (size + 31) // 32 * 32
        return nc.alloc_sbuf_tensor_at(name, shape, dt, offset=offset)

    def region(kib):
        at = cursor[0]
        cursor[0] += kib * KIB
        return at

    r_h, r_y, r_qv, r_hi, r_lo = region(32), region(32), region(16), region(16), region(16)
    h_hi = place("h_hi", [P, KB_D, NT], F32R, at=r_h)
    h_lo = place("h_lo", [P, KB_D, NT], F32R, at=r_h + 16 * KIB)
    y_hi = place("y_hi", [P, 8, NT], F32R, at=r_y)
    y_lo = place("y_lo", [P, 8, NT], F32R, at=r_y + 16 * KIB)
    probs = place("probs", [P, 2, A_GROUP, 256], at=r_y + 8 * KIB)
    probsT = place("probsT", [P, 2, 2, A_GROUP, P], at=r_y + 24 * KIB)
    res = place("res", [P, TB, D], at=r_y)
    squares = place("squares", [P, D], at=r_y + 16 * KIB)
    qT = place("qT", [P, 4, NT], at=r_qv)
    vb = place("vb", [P, TB, 512], at=r_qv + 8 * KIB)
    gate_a = place("gate_a", [P, 4, NT], at=r_qv)
    gate_b = place("gate_b", [P, 4, NT], at=r_qv + 8 * KIB)
    xn = place("xn", [P, TB, D], at=r_qv)
    ya = place("ya", [P, TB, 512], at=r_hi)
    yb = place("yb", [P, TB, 512], at=r_hi + 8 * KIB)
    m_hi = place("m_hi", [P, KB_D, NT], F32R, at=r_hi)
    qbT = place("qbT", [P, 2, NT], at=r_lo)
    kb = place("kb", [P, TB, 256], at=r_lo + 4 * KIB)
    la = place("la", [P, TB, 256], at=r_lo + 8 * KIB)
    lscr = place("lscr", [P, TB, 256], at=r_lo + 12 * KIB)
    m_lo = place("m_lo", [P, KB_D, NT], F32R, at=r_lo)
    ada_ss = [place(f"ada_ss{k}", [P, 2 * D], at=(r_h if k < 4 else r_y) + 8 * KIB * (k % 4)) for k in range(KB_D)]
    ada_gt = [place(f"ada_gt{k}", [P, D], at=r_hi + 4 * KIB * k) for k in range(KB_D)]

    w_split = place("w_split_hi", [P, RING, 2, 512], F32R)
    w_split_lo = place("w_split_lo", [P, RING, 2, 512], F32R)
    stage = [place(f"stage{i}", [P, 2, 512]) for i in range(STAGES)]
    kT = place("kT", [P, CHUNK + NT])
    v = place("v", [P, 1 + TB, P])
    state = place("state", [P, 4, 256])
    dist = place("dist", [P, 2, WIN])
    ident = place("ident", [P, P])
    suffix = place("suffix", [P, P])
    chunks = place("chunks", [P, 2])
    gate_row = place("gate_row", [P, D])
    final_row = place("final_row", [P, D])
    w_al = place("w_al", [RANK + 1, 256])
    zaT = place("zaT", [RANK + 1, NT])
    za = place("za", [P, TB, RANK])
    ones = place("ones", [P, P], at=cursor[0])
    tmp = place("tmp", [P, 2, 512])
    tmp2 = place("tmp2", [P, 2, 512])
    small = place("small", [P, 336])
    assert cursor[0] <= nc.sbuf_usable_end, cursor[0]

    used = [0]

    def cell(n):
        a = used[0]
        used[0] += n
        return small[:, a:a + n]

    c_col, c_tanh, c_silu = cell(8), cell(8), cell(8)
    shift, gscale, modb, norm_col = cell(8), cell(8), cell(16), cell(8)
    half_g, sink8 = cell(1), cell(8)
    maxs, nmax, esink, sums, rden = (cell(32).rearrange("p (u j) -> p u j", j=4) for _ in range(5))
    decay = cell(16)
    ssq_x, ssq_o, ssq_f = cell(4), cell(16), cell(4)
    rs_x, rs_o, rs_f = cell(4), cell(16), cell(4)
    rs_m, rs_t = cell(16), cell(16)
    assert used[0] <= 336, used

    def psum(name, shape):
        return nc.alloc_psum_tensor(name, shape, F32)

    acc = [psum(f"acc{i}", [P, 512]) for i in range(2)]
    ps_s = psum("ps_s", [P, 4, 256])
    ps_t = psum("ps_t", [P, 2, 512])
    ps_y = psum("ps_y", [P, 512])
    ps_o = psum("ps_o", [P, 512])

    names = """consts_loaded c_loaded stored
        w_ready w_used acc_full
        c_tanh_done ss_summed gt_summed mod_full gate_full gate_ready
        x_squared x_scaled xT_full xT_plain h_hi_ready h_ready
        gate_tanh vT_full v_ready
        scores_full scores_read negmax probs_ready ptrans_full ptrans_act ptrans_dve pv_full y_scaled
        zaT_full zaT_ready z_full log_ready la_ready cum_full decay_ready kb_ready kv_full state_ready
        o_full o_squared o_gated yb_ready yT_full yT_hi_ready yT_ready
        m_plain m_hi_ready m_ready res_ready res_squared result_ready
        dve_step act_step pool_step pe_turn pool_turn""".split()
    S = {n: nc.alloc_semaphore(n) for n in names}
    acc_free = [nc.alloc_semaphore(f"acc_free{i}") for i in range(2)]
    x_loaded = [nc.alloc_semaphore(f"x_loaded{i}") for i in range(TB)]
    res_loaded = [nc.alloc_semaphore(f"res_loaded{i}") for i in range(TB)]
    ss_loaded = [nc.alloc_semaphore(f"ss_loaded{k}") for k in range(KB_D)]
    gt_loaded = [nc.alloc_semaphore(f"gt_loaded{k}") for k in range(KB_D)]
    stage_loaded = [nc.alloc_semaphore(f"stage_loaded{i}") for i in range(STAGES)]
    (consts_loaded, c_loaded, stored,
     w_ready, w_used, acc_full,
     c_tanh_done, ss_summed, gt_summed, mod_full, gate_full, gate_ready,
     x_squared, x_scaled, xT_full, xT_plain, h_hi_ready, h_ready,
     gate_tanh, vT_full, v_ready,
     scores_full, scores_read, negmax, probs_ready, ptrans_full, ptrans_act, ptrans_dve, pv_full, y_scaled,
     zaT_full, zaT_ready, z_full, log_ready, la_ready, cum_full, decay_ready, kb_ready, kv_full, state_ready,
     o_full, o_squared, o_gated, yb_ready, yT_full, yT_hi_ready, yT_ready,
     m_plain, m_hi_ready, m_ready, res_ready, res_squared, result_ready,
     dve_step, act_step, pool_step, pe_turn, pool_turn) = (S[n] for n in names)

    CONSTS = 12
    def may_fill(t, f):
        return t * (FILLS // 2) + (f // 2 + 1)

    def filled(t, f):
        return t * FILLS + (f + 1)

    def w_src(panel, duo):
        matrix = PANELS[panel][0]
        if matrix == "w_br":
            return (w_br_a if duo < 2 else w_br_b), 2 * P * (duo % 2)
        return (w_in if matrix == "w_in" else w_out), 2 * P * duo

    loads_of = [len(PANELS[d // 4][1]) for d in range(DUOS)]
    loads_upto = [sum(n for e, n in enumerate(loads_of[:d + 1]) if e % STAGES == d % STAGES) for d in range(DUOS)]
    loads_tile = [sum(n for e, n in enumerate(loads_of) if e % STAGES == i) for i in range(STAGES)]

    def x_block(t, i):
        return x[bass.ds(t * NT + i * P, P), :]

    block = nc.Block()
    with block:
        @block.sync
        def _(sp):
            sp.dma_start(c_col, c).then_inc(c_loaded, 16)
            for i in range(TB):
                sp.dma_start(xn[:, i, :], x[i * P:(i + 1) * P, :]).then_inc(x_loaded[i], 16)
            for k in range(KB_D):
                sp.dma_start(ada_ss[k][:], ada_w[k * P:(k + 1) * P, 0:2 * D]).then_inc(ss_loaded[k], 16)
            for k in range(KB_D):
                sp.dma_start(ada_gt[k][:], ada_w[k * P:(k + 1) * P, 2 * D:3 * D]).then_inc(gt_loaded[k], 16)
            with sp.Fori(0, TILES) as t:
                for d in range(DUOS):
                    sp.wait_ge(w_ready, t * DUOS + (d + 1))
                    src, row = w_src(d // 4, d % 4)
                    col = 0
                    for first, n in PANELS[d // 4][1]:
                        sp.dma_start(stage[d % STAGES][:, :, col:col + n],
                                     src[row:row + 2 * P, first:first + n].rearrange("(k p) n -> p k n", p=P)
                                     ).then_inc(stage_loaded[d % STAGES], 16)
                        col += n
            for xl in x_loaded:
                sp.wait_ge(xl, 16 * (TILES + 1))
            sp.wait_ge(stored, 16 + 16 * TB * TILES)

        @block.gpsimd
        def _(pool):
            pool.sem_inc(w_ready, STAGES)
            with pool.Fori(0, TILES) as t:
                for d in range(DUOS):
                    n, r, s = WIDTH[d // 4], d % RING, d % STAGES
                    pool.wait_ge(stage_loaded[s], t * (16 * loads_tile[s]) + 16 * loads_upto[d])
                    pool.wait_ge(w_used, t * DUOS + (d + 1))
                    pool.sem_inc(pool_turn, 1)
                    if d // 4 == P_QA:
                        def split_as(z, k):
                            return z[:, r, k, :].rearrange("p (j g e) -> p j g e", g=2, j=4)
                        parts = [(split_as(w_split, k), split_as(w_split_lo, k),
                                  stage[s][:, k, :].rearrange("p (g j e) -> p j g e", g=2, j=4)) for k in range(2)]
                    else:
                        parts = [(w_split[:, r, :, :n], w_split_lo[:, r, :, :n], stage[s][:, :, :n])]
                    for hi, _, raw in parts:
                        last = nc.gpsimd.tensor_scalar(hi, raw, 1.0, 1.0, ALU.mult, ALU.mult)
                    last.then_inc(pool_step, 1)
                    pool.wait_ge(pool_step, t * DUOS + (d + 1))
                    for hi, lo, raw in parts:
                        last = nc.gpsimd.tensor_tensor(lo, raw, hi.bitcast(F32), ALU.subtract)
                    last.then_inc(w_ready, 1)

        @block.tensor
        def _(pe):
            mm = nc.tensor.matmul

            def x_transpose(T, k):
                if k == 0:
                    pe.wait_ge(x_scaled, T + 1)
                if k >= 2:
                    pe.wait_ge(xT_plain, T * KB_D + (k - 1))
                for i in range(TB):
                    last = nc.tensor.transpose(ps_t[:, k % 2, i * P:(i + 1) * P], xn[:, i, k * P:(k + 1) * P], ident[:])
                last.then_inc(xT_full, 1)

            pe.sem_inc(w_used, RING - 1)
            pe.wait_ge(consts_loaded, 16 * CONSTS)
            pe.wait_ge(ss_summed, 1)
            for j in range(16):
                last = mm(acc[0][:, j:j + 1], ada_ss[0][:, j * P:(j + 1) * P], ones[:, 0:1], start=True, stop=True)
            last.then_inc(mod_full, 1)
            for k in range(KB_D):
                x_transpose(0, k)
            pe.wait_ge(gt_summed, 1)
            for half in range(2):
                if half:
                    pe.wait_ge(gate_ready, 1)
                mm(acc[1][:], ones[:], ada_gt[0][:, half * 512:half * 512 + 512], start=True, stop=True
                   ).then_inc(gate_full, 1)

            with pe.Fori(0, TILES) as t:
                def three(o, a_hi, a_lo, b_hi, b_lo, start, stop):
                    first = mm(o, a_hi, b_hi, start=start, stop=False)
                    mm(o, a_hi, b_lo, start=False, stop=False)
                    return first, mm(o, a_lo, b_hi, start=False, stop=stop)

                def weights(panel, k, cols):
                    r = (4 * panel + k // 2) % RING
                    return w_split[:, r, k % 2, cols], w_split_lo[:, r, k % 2, cols]

                def fill(f, panel, ks, first, last_fill, step, ready=None):
                    pe.wait_ge(acc_free[f % 2], may_fill(t, f))
                    for k in ks:
                        duo = 4 * panel + k // 2
                        if first and k % 2 == 0:
                            pe.wait_ge(w_ready, t * DUOS + (duo + 1 + STAGES))
                        if ready is not None and k == ks[0] or ready is not None and ready[2]:
                            pe.wait_ge(ready[0], t * 8 + ready[1](k))
                        product, last = step(k, k == ks[0], k == ks[-1])
                        if first and k == 0:
                            product.then_inc(w_used, 1)
                        if last_fill and k % 2 and k != ks[-1]:
                            last.then_inc(w_used, 1)
                        if last_fill and k == 4 and ks[0] == 4:
                            product.then_inc(w_used, 1)
                    last.then_inc(acc_full, 1)

                def transposed(panel, f, c0, b, ks, first, last_fill, ready=None):
                    b_hi, b_lo = b

                    def step(k, start, stop):
                        w_hi, w_lo = weights(panel, k, slice(c0, c0 + P))
                        return three(acc[f % 2][:], w_hi, w_lo, b_hi[:, k, :], b_lo[:, k, :], start, stop)

                    fill(f, panel, ks, first, last_fill, step, ready)

                def by_token(panel, f, i, n, a, first, last_fill, ready=None):
                    a_hi, a_lo = a
                    tok = slice(i * P, (i + 1) * P)

                    def step(k, start, stop):
                        w_hi, w_lo = weights(panel, k, slice(0, n))
                        return three(acc[f % 2][:, :n], a_hi[:, k, tok], a_lo[:, k, tok], w_hi, w_lo, start, stop)

                    fill(f, panel, ks_all, first, last_fill, step, ready)

                def evacuated(f):
                    pe.wait_ge(acc_free[f % 2], may_fill(t, f) + 1)

                ks_all = list(range(KB_D))
                h = (h_hi, h_lo)

                def dense(s):
                    panel, b = s // 4, s % 4
                    f = first_fill(s)
                    first, last_fill = b == 0, b == 3
                    if panel == P_QA:
                        transposed(panel, f, b * P, h, ks_all, first, last_fill,
                                   ready=(h_ready, lambda k: k + 1, True) if first else None)
                    elif panel == P_KVQ:
                        transposed(panel, f, b * P, h, ks_all, first, last_fill)
                    elif panel in (P_GA, P_KZ, P_VB, P_GB):
                        by_token(panel, f, b, WIDTH[panel], h, first, last_fill)
                    elif panel in P_ZM:
                        transposed(panel, f, b * P, h, ks_all, first, last_fill)
                    elif panel in P_BR:
                        y = (y_hi, y_lo)
                        pair = P_BR.index(panel) == 0 and first
                        transposed(panel, f, b * P, y, ks_all[:4], first, last_fill,
                                   ready=(yT_ready, lambda k: 4, False) if pair else None)
                        transposed(panel, f + 1, b * P, y, ks_all[4:], first, last_fill,
                                   ready=(yT_ready, lambda k: 8, False) if pair else None)
                    else:
                        by_token(panel, f, b, 512, (m_hi, m_lo), first, last_fill,
                                 ready=(m_ready, lambda k: k + 1, True) if panel == P_OUT[0] and first else None)

                def scores(u):
                    pair, g = u // 2, u % 2
                    if u == 0:
                        evacuated(2)
                        evacuated(3)
                        evacuated(first_fill(4 * P_KVQ))
                    else:
                        pe.wait_ge(scores_read, t * 8 + u)
                    rows = slice(g * A_DIM, (g + 1) * A_DIM)
                    for j in range(A_GROUP):
                        last = mm(ps_s[:, j, 0:WIN], qT[rows, j, pair * P:(pair + 1) * P],
                                  kT[rows, pair * P:pair * P + WIN], start=True, stop=True)
                    last.then_inc(scores_full, 1)

                def v_transpose():
                    evacuated(first_fill(4 * P_KVQ + 1))
                    for i in range(TB):
                        last = nc.tensor.transpose(ps_t[:, 0, i * P:(i + 1) * P], tmp2[:, 0, i * P:(i + 1) * P], ident[:])
                    last.then_inc(vT_full, 1)

                def transpose_probs(u):
                    pe.wait_ge(probs_ready, t * 8 + (u + 1))
                    if u == 0:
                        pe.wait_ge(v_ready, t + 1)
                    if u:
                        pe.wait_ge(ptrans_act, t * 8 + u)
                        pe.wait_ge(ptrans_dve, t * 8 + u)
                    for half, c0 in ((0, P), (1, 0)):
                        for j in range(A_GROUP):
                            last = nc.tensor.transpose(ps_t[:, half, j * P:(j + 1) * P],
                                                       probs[:, u % 2, j, c0:c0 + P], ident[:])
                    last.then_inc(ptrans_full, 1)

                def attend(u):
                    pair, g = u // 2, u % 2
                    if u == 0:
                        pe.wait_ge(v_ready, t + 1)
                    else:
                        pe.wait_ge(y_scaled, t * 8 + u)
                    pe.wait_ge(ptrans_act, t * 8 + (u + 1))
                    pe.wait_ge(ptrans_dve, t * 8 + (u + 1))
                    vc = slice(g * A_DIM, (g + 1) * A_DIM)
                    for j in range(A_GROUP):
                        o = ps_y[:, j * A_DIM:(j + 1) * A_DIM]
                        mm(o, probsT[:, u % 2, 0, j, :], v[:, pair + 1, vc], start=True, stop=False)
                        last = mm(o, probsT[CHUNK:P, u % 2, 1, j, :], v[CHUNK:P, pair, vc], start=False, stop=True)
                    last.then_inc(pv_full, 1)

                def y_transpose(n):
                    if n == 0:
                        pe.wait_ge(y_scaled, t * 8 + 8)
                    if n == 4:
                        pe.wait_ge(yb_ready, t + 1)
                    if n >= 2:
                        pe.wait_ge(yT_ready, t * 8 + (n - 1))
                    src = ya if n < 4 else yb
                    for i in range(TB):
                        last = nc.tensor.transpose(ps_t[:, n % 2, i * P:(i + 1) * P],
                                                   src[:, i, (n % 4) * P:(n % 4 + 1) * P], ident[:])
                    last.then_inc(yT_full, 1)

                def za_transpose():
                    evacuated(first_fill(4 * P_KZ + 2))
                    evacuated(first_fill(4 * P_KZ + 3))
                    for i in range(TB):
                        last = nc.tensor.transpose(ps_t[0:RANK, 0, i * P:(i + 1) * P], za[:, i, :], ident[:])
                    last.then_inc(zaT_full, 1)

                def decay_logits():
                    pe.wait_ge(zaT_ready, t + 1)
                    pe.wait_ge(scores_read, t * 8 + 8)
                    for i in range(TB):
                        last = mm(ps_s[:, i, :], zaT[:, i * P:(i + 1) * P], w_al[:], start=True, stop=True)
                    last.then_inc(z_full, 1)

                def suffix_sums():
                    pe.wait_ge(la_ready, t + 1)
                    pe.wait_ge(y_scaled, t * 8 + 8)
                    for i in range(TB):
                        mm(ps_s[:, i, :], suffix[:], la[:, i, :], start=True, stop=True)
                    for i in range(TB):
                        for hp in range(2):
                            a = hp * 8 + 2 * i
                            last = mm(ps_y[:, a:a + 2], la[:, i, hp * P:(hp + 1) * P], chunks[:], start=True, stop=True)
                    last.then_inc(cum_full, 1)

                def key_values(i):
                    if i == 0:
                        pe.wait_ge(kb_ready, t + 1)
                        evacuated(first_fill(4 * P_VB + 2))
                        evacuated(first_fill(4 * P_VB + 3))
                    else:
                        pe.wait_ge(state_ready, t * 4 + i)
                    pe.sem_inc(pe_turn, 1)
                    for c2 in range(2):
                        rows = slice(c2 * CHUNK, (c2 + 1) * CHUNK)
                        for hd in range(B_HEADS):
                            hp, low = hd // 2, hd % 2
                            last = mm(ps_s[low * B_K:(low + 1) * B_K, 2 * c2, hp * P:(hp + 1) * P], kb[rows, i, hd * B_K:(hd + 1) * B_K],
                                      vb[rows, i, hd * B_V:(hd + 1) * B_V], start=True, stop=True)
                    last.then_inc(kv_full, 1)

                def read_state(i):
                    pe.wait_ge(state_ready, t * 4 + (i + 1))
                    if i == 0:
                        evacuated(first_fill(4 * P_KVQ + 2))
                        evacuated(first_fill(4 * P_KVQ + 3))
                    else:
                        pe.wait_ge(o_gated, t * 4 + i)
                    pe.sem_inc(pe_turn, 1)
                    for c2 in range(2):
                        tok = slice(i * P + c2 * CHUNK, i * P + (c2 + 1) * CHUNK)
                        for hd in range(B_HEADS):
                            hp, low = hd // 2, hd % 2
                            rows = slice(low * B_K, (low + 1) * B_K)
                            last = mm((ps_o, ps_y)[low][c2 * CHUNK:(c2 + 1) * CHUNK, hp * B_V:(hp + 1) * B_V],
                                      qbT[rows, hp, tok], state[rows, (2 * i + c2) % 4, hp * P:(hp + 1) * P],
                                      start=True, stop=True)
                    last.then_inc(o_full, 1)

                for s in range(SLOTS):
                    dense(s)
                    if 0 <= s - 9 < 8:
                        attend(s - 9)
                    if 0 <= s - 8 < 8:
                        transpose_probs(s - 8)
                    if 0 <= s - 7 < 8:
                        scores(s - 7)
                    if s == 6:
                        v_transpose()
                    if s == 16:
                        za_transpose()
                    if s == 17:
                        decay_logits()
                    if s == 19:
                        suffix_sums()
                    if 20 <= s < 24:
                        y_transpose(s - 20)
                        key_values(s - 20)
                    if 21 <= s < 25:
                        read_state(s - 21)
                    if 27 <= s < 31:
                        y_transpose(s - 23)
                    if 52 <= s:
                        x_transpose(t + 1, 2 * (s - 52))
                        x_transpose(t + 1, 2 * (s - 52) + 1)

        @block.vector
        def _(dve):
            V = nc.vector
            steps = [0]
            DVE_BEFORE, DVE_TILE = 36, 97

            def link(ins, t=None):
                ins.then_inc(dve_step, 1)
                steps[0] += 1
                if t is None:
                    dve.wait_ge(dve_step, steps[0])
                else:
                    dve.wait_ge(dve_step, t * DVE_TILE + (DVE_BEFORE + steps[0]))

            def rsqrt(out_, sq, n, count, t):
                m, a = rs_m[:, :count], rs_t[:, :count]
                link(V.tensor_scalar(m, sq, 1.0 / n, EPS, ALU.mult, ALU.add), t)
                link(V.tensor_scalar(a.bitcast(I32), m.bitcast(I32), 1, None, ALU.logical_shift_right), t)
                link(V.tensor_scalar(out_.bitcast(I32), a.bitcast(I32), -1.0, float(RSQRT_MAGIC), ALU.mult, ALU.add), t)
                for _ in range(3):
                    link(V.tensor_tensor(a, out_, out_, ALU.mult), t)
                    link(V.tensor_tensor(a, a, m, ALU.mult), t)
                    link(V.tensor_scalar(a, a, -0.5, 1.5, ALU.mult, ALU.add), t)
                    link(V.tensor_tensor(out_, out_, a, ALU.mult), t)

            def x_scale(T, t):
                dve.wait_ge(x_squared, T + 1)
                rsqrt(rs_x, ssq_x, D, TB, t)
                for i in range(TB):
                    last = V.tensor_scalar(xn[:, i, :], xn[:, i, :], rs_x[:, i:i + 1], None, ALU.mult)
                last.then_inc(x_scaled, 1)

            def modulate(T, k):
                for kk in (k, k + 1):
                    if kk >= 2:
                        dve.wait_ge(h_ready, T * KB_D + (kk - 1))
                    dve.wait_ge(xT_full, T * KB_D + (kk + 1))
                    V.tensor_scalar(tmp2[:, kk % 2, :], ps_t[:, kk % 2, :], gscale[:, kk:kk + 1], shift[:, kk:kk + 1],
                                    ALU.mult, ALU.add).then_inc(xT_plain, 1)
                for kk in (k, k + 1):
                    dve.wait_ge(h_hi_ready, T * KB_D + (kk + 1))
                    V.tensor_tensor(h_lo[:, kk, :], tmp2[:, kk % 2, :], h_hi[:, kk, :].bitcast(F32),
                                    ALU.subtract).then_inc(h_ready, 1)

            V.memset(kT[:, 0:CHUNK], 0.0)
            V.memset(v[:, 0, :], 0.0)
            V.memset(state[:, 3, :], 0.0)
            V.memset(zaT[:], 1.0)
            dve.wait_ge(c_tanh_done, 1)
            link(V.scalar_tensor_tensor(c_silu, c_tanh, 1.0, c_col, ALU.add, ALU.mult))
            link(V.tensor_scalar(c_silu, c_silu, 0.5, None, ALU.mult))
            V.memset(ones[:], 1.0)

            def weigh(parts, loaded):
                for k in range(KB_D):
                    dve.wait_ge(loaded[k], 16)
                    if k == 0:
                        link(V.tensor_scalar(parts[0][:], parts[0][:], c_silu[:, 0:1], None, ALU.mult))
                    elif k < KB_D - 1:
                        link(V.scalar_tensor_tensor(parts[0][:], parts[k][:], c_silu[:, k:k + 1], parts[0][:],
                                                    ALU.mult, ALU.add))
                    else:
                        last = V.scalar_tensor_tensor(parts[0][:], parts[k][:], c_silu[:, k:k + 1], parts[0][:],
                                                      ALU.mult, ALU.add)
                return last

            weigh(ada_ss, ss_loaded).then_inc(ss_summed, 1)
            dve.wait_ge(consts_loaded, 16 * CONSTS)
            link(V.tensor_scalar(sink8, sink8, SINK_SCALE, None, ALU.mult))
            link(V.tensor_scalar(half_g, half_g, 0.5, None, ALU.mult))
            x_scale(0, None)
            dve.wait_ge(mod_full, 1)
            V.tensor_tensor(shift, acc[0][:, 0:8], modb[:, 0:8], ALU.add)
            link(V.tensor_tensor(gscale, acc[0][:, 8:16], modb[:, 8:16], ALU.add))
            link(V.scalar_tensor_tensor(gscale, gscale, 1.0, norm_col, ALU.add, ALU.mult))
            dve.sem_inc(acc_free[0], 1)
            for k in range(0, KB_D, 2):
                modulate(0, k)
            weigh(ada_gt, gt_loaded).then_inc(gt_summed, 1)
            for half in range(2):
                cols = slice(half * 512, half * 512 + 512)
                dve.wait_ge(gate_full, half + 1)
                V.tensor_tensor(gate_row[:, cols], gate_row[:, cols], acc[1][:], ALU.add).then_inc(gate_ready, 1)
            dve.wait_ge(gate_ready, 2)
            dve.sem_inc(acc_free[1], 1)
            link(V.tensor_scalar(gate_row[:], gate_row[:], 0.5, None, ALU.mult))
            assert steps[0] == DVE_BEFORE, steps
            steps[0] = 0

            with dve.Fori(0, TILES) as t:
                def freed(f):
                    dve.wait_ge(acc_free[f % 2], may_fill(t, f) + 1)

                def gate(f, b, out_):
                    dve.wait_ge(gate_tanh, t * 8 + (b + 1))
                    V.scalar_tensor_tensor(out_, tmp[:, b % 2, :], 1.0, acc[f % 2][:], ALU.add, ALU.mult
                                           ).then_inc(acc_free[f % 2], 1)

                def bias_and_max(u):
                    pair, g, b = u // 2, u % 2, u % 2
                    dve.wait_ge(scores_full, t * 8 + (u + 1))
                    for j in range(A_GROUP):
                        slope = 2.0 ** -(A_GROUP * g + j + 1)
                        last = V.scalar_tensor_tensor(probs[:, b, j, CHUNK:256], dist[:, 1 if pair else 0, :],
                                                      -SINK_SCALE * slope, ps_s[:, j, 0:WIN], ALU.mult, ALU.add)
                    last.then_inc(scores_read, 1)
                    dve.wait_ge(scores_read, t * 8 + (u + 1))
                    link(V.tensor_reduce(out=maxs[:, u, :], in_=probs[:, b, :, CHUNK:256], op=ALU.max, axis=AX.X), t)
                    link(V.tensor_tensor(maxs[:, u, :], maxs[:, u, :], sink8[:, 4 * g:4 * g + 4], ALU.max), t)
                    V.tensor_tensor(esink[:, u, :], sink8[:, 4 * g:4 * g + 4], maxs[:, u, :], ALU.subtract)
                    V.tensor_scalar(nmax[:, u, :], maxs[:, u, :], -1.0 / SINK_SCALE, None, ALU.mult).then_inc(negmax, 1)

                def denominators(u):
                    dve.wait_ge(probs_ready, t * 8 + (u + 1))
                    link(V.tensor_tensor(sums[:, u, :], sums[:, u, :], esink[:, u, :], ALU.add), t)
                    link(V.reciprocal(rden[:, u, :], sums[:, u, :]), t)
                    dve.wait_ge(ptrans_full, t * 8 + (u + 1))
                    V.tensor_copy(probsT[CHUNK:P, u % 2, 1, :, :].rearrange("p j q -> p (j q)"),
                                  ps_t[CHUNK:P, 1, :]).then_inc(ptrans_dve, 1)

                def scale_and_gate(u):
                    pair, g = u // 2, u % 2
                    if g == 0:
                        freed(first_fill(4 * P_GA + pair))
                    dve.wait_ge(pv_full, t * 8 + (u + 1))
                    for j in range(A_GROUP):
                        cols = slice((A_GROUP * g + j) * A_DIM, (A_GROUP * g + j + 1) * A_DIM)
                        last = V.scalar_tensor_tensor(ya[:, pair, cols], ps_y[:, j * A_DIM:(j + 1) * A_DIM],
                                                      rden[:, u, j:j + 1], ya[:, pair, cols], ALU.mult, ALU.mult)
                    last.then_inc(y_scaled, 1)

                def y_low(n):
                    dve.wait_ge(yT_hi_ready, t * 8 + (n + 1))
                    V.scalar_tensor_tensor(y_lo[:, n, :], ps_t[:, n % 2, :], 0.5 if n < 4 else half_g,
                                           y_hi[:, n, :].bitcast(F32), ALU.mult, ALU.subtract).then_inc(yT_ready, 1)

                def update_state(i):
                    dve.wait_ge(kv_full, t * 4 + (i + 1))
                    for c2 in range(2):
                        ch = 2 * i + c2
                        for hp in range(2):
                            cols = slice(hp * P, (hp + 1) * P)
                            last = V.scalar_tensor_tensor(state[:, ch % 4, cols], state[:, (ch - 1) % 4, cols],
                                                          decay[:, hp * 8 + ch:hp * 8 + ch + 1],
                                                          ps_s[:, 2 * c2, cols],
                                                          ALU.mult, ALU.add)
                        if c2 == 0:
                            link(last, t)
                    last.then_inc(state_ready, 1)
                    dve.wait_ge(state_ready, t * 4 + (i + 1))

                def normalise(blocks):
                    i0, n = blocks[0], len(blocks)
                    dve.wait_ge(res_squared, t * 4 + (i0 + n))
                    rsqrt(rs_f[:, i0:i0 + n], ssq_f[:, i0:i0 + n], D, n, t)
                    for i in blocks:
                        V.scalar_tensor_tensor(res[:, i, :], res[:, i, :], rs_f[:, i:i + 1], final_row[:],
                                               ALU.mult, ALU.mult).then_inc(result_ready, 1)

                def merge(s, q, j):
                    f, n = first_fill(s), 4 * q + j
                    if j == 0:
                        freed(first_fill(4 * P_ZM[2 * q + 1] + 2))
                        freed(first_fill(4 * P_ZM[2 * q + 1] + 3))
                    if n >= 2:
                        dve.wait_ge(m_ready, t * 8 + (n - 1))
                    dve.wait_ge(acc_full, filled(t, f))
                    V.scalar_tensor_tensor(tmp[:, j % 2, :], gate_a[:, j, :], 1.0, acc[f % 2][:], ALU.add, ALU.mult
                                           ).then_inc(acc_free[f % 2], 1)
                    dve.wait_ge(acc_full, filled(t, f + 1))
                    V.scalar_tensor_tensor(tmp2[:, j % 2, :], gate_b[:, j, :], 1.0, acc[(f + 1) % 2][:], ALU.add, ALU.mult
                                           ).then_inc(acc_free[(f + 1) % 2], 1)
                    freed(f)
                    freed(f + 1)
                    V.tensor_tensor(tmp[:, j % 2, :], tmp[:, j % 2, :], tmp2[:, j % 2, :], ALU.add).then_inc(m_plain, 1)
                    dve.wait_ge(m_hi_ready, t * 8 + (n + 1))
                    V.tensor_tensor(m_lo[:, n, :], tmp[:, j % 2, :], m_hi[:, n, :].bitcast(F32), ALU.subtract
                                    ).then_inc(m_ready, 1)

                for s in range(SLOTS):
                    panel, b = s // 4, s % 4
                    f = first_fill(s)
                    a = acc[f % 2]
                    if panel == P_KVQ and b < 2 or panel == P_KZ:
                        dve.wait_ge(acc_full, filled(t, f))
                    if panel == P_KVQ and b == 0:
                        V.tensor_copy(kT[:, CHUNK:], a[:]).then_inc(acc_free[f % 2], 1)
                    if panel == P_KVQ and b == 1:
                        dve.wait_ge(h_ready, t * 8 + 8)
                        V.tensor_copy(tmp2[:, 0, :], a[:]).then_inc(acc_free[f % 2], 1)
                    if panel == P_KZ:
                        V.tensor_copy(kb[:, b, :], a[:, 0:256])
                        V.tensor_copy(za[:, b, :], a[:, 256:256 + RANK]).then_inc(acc_free[f % 2], 1)
                    if panel == P_GA:
                        gate(f, b, ya[:, b, :])
                    if panel == P_GB:
                        gate(f, 4 + b, yb[:, b, :])
                    if s == 6:
                        dve.wait_ge(vT_full, t + 1)
                        V.tensor_copy(v[:, 1:, :].rearrange("p i c -> p (i c)"), ps_t[:, 0, :]).then_inc(v_ready, 1)
                        dve.wait_ge(stored, t * (16 * TB) + 16)
                        V.memset(probs[:, :, :, 0:CHUNK], 0.0)
                    if 0 <= s - 9 < 8:
                        scale_and_gate(s - 9)
                    if 0 <= s - 8 < 8:
                        denominators(s - 8)
                    if 0 <= s - 7 < 8:
                        bias_and_max(s - 7)
                    if s == 16:
                        dve.wait_ge(zaT_full, t + 1)
                        V.tensor_copy(zaT[0:RANK, :], ps_t[0:RANK, 0, :]).then_inc(zaT_ready, 1)
                    if s == 18:
                        dve.wait_ge(log_ready, t + 1)
                        V.scalar_tensor_tensor(la[:], ps_s[:], 0.0, lscr[:], ALU.min, ALU.subtract).then_inc(la_ready, 1)
                        V.tensor_copy(kT[:, 0:CHUNK], kT[:, NT:NT + CHUNK])
                        V.tensor_copy(v[:, 0, :], v[:, TB, :])
                        link(V.tensor_copy(dist[:, 0, :], dist[:, 1, :]), t)
                    if s == 19:
                        dve.wait_ge(decay_ready, t + 1)
                        V.tensor_tensor(kb[:], kb[:], lscr[:], ALU.mult).then_inc(kb_ready, 1)
                    if 20 <= s < 24:
                        update_state(s - 20)
                        y_low(s - 20)
                    if 21 <= s < 25:
                        i = s - 21
                        freed(first_fill(4 * P_GB + i))
                        dve.wait_ge(o_squared, t * 4 + (i + 1))
                        for low, o in enumerate((ps_o, ps_y)):
                            heads = yb[:, i, :].rearrange("p (h l e) -> p l h e", l=2, e=B_V)[:, low]
                            last = V.tensor_tensor(heads, heads, o[:, 0:256].rearrange("p (h e) -> p h e", e=B_V), ALU.mult)
                        last.then_inc(o_gated, 1)
                    if s == 25:
                        dve.wait_ge(o_squared, t * 4 + 4)
                        rsqrt(rs_o, ssq_o, B_V, 4 * TB, t)
                        dve.wait_ge(o_gated, t * 4 + 4)
                        yb3 = yb[:].rearrange("p i (h e) -> p (i h) e", e=B_V)
                        V.tensor_tensor(yb3, yb3, rs_o.unsqueeze(2).to_broadcast([P, 4 * TB, B_V]), ALU.mult
                                        ).then_inc(yb_ready, 1)
                    if 27 <= s < 31:
                        y_low(s - 23)
                    if panel in P_BR:
                        merge(s, P_BR.index(panel), b)
                    if panel in P_OUT:
                        cols = slice(P_OUT.index(panel) * 512, P_OUT.index(panel) * 512 + 512)
                        if panel == P_OUT[0]:
                            dve.wait_ge(res_loaded[b], t * 16 + 16)
                        n = 4 * P_OUT.index(panel) + b
                        if n >= 2:
                            dve.wait_ge(res_ready, t * 8 + (n - 1))
                        dve.wait_ge(acc_full, filled(t, f))
                        V.tensor_tensor(tmp[:, b % 2, :], a[:], gate_row[:, cols], ALU.mult).then_inc(acc_free[f % 2], 1)
                        freed(f)
                        V.tensor_tensor(res[:, b, cols], res[:, b, cols], tmp[:, b % 2, :], ALU.add).then_inc(res_ready, 1)
                    if s == 51:
                        x_scale(t + 1, t)
                    if s >= 52:
                        modulate(t + 1, 2 * (s - 52))
                    if s == 54:
                        normalise((0, 1))
                    if s == 55:
                        normalise((2, 3))
                assert steps[0] == DVE_TILE, steps

        @block.scalar
        def _(act):
            A = nc.scalar.activation
            steps = [0]
            ACT_BEFORE, ACT_TILE = 3, 5

            def link(ins, t=None):
                ins.then_inc(act_step, 1)
                steps[0] += 1
                if t is None:
                    act.wait_ge(act_step, steps[0])
                else:
                    act.wait_ge(act_step, t * ACT_TILE + (ACT_BEFORE + steps[0]))

            act.sem_inc(stored, 16)
            for dst, src in ((modb, ada_b), (norm_col, norm_g), (half_g, head_g),
                             (sink8, sinks.partition_broadcast(P)),
                             (ident[:], ident_in), (suffix[:], suffix_in), (chunks[:], chunks_in), (dist[:], dist_in),
                             (gate_row[:], ada_b_row.partition_broadcast(P)),
                             (final_row[:], final_g.partition_broadcast(P))):
                act.dma_start(dst, src).then_inc(consts_loaded, 16)
            act.dma_start(w_al[0:RANK, :], w_alpha).then_inc(consts_loaded, 16)
            act.dma_start(w_al[RANK:RANK + 1, :], b_alpha).then_inc(consts_loaded, 16)
            act.wait_ge(c_loaded, 16)
            A(c_tanh, c_col, ACT.Tanh, scale=0.5).then_inc(c_tanh_done, 1)

            def x_square(T, t, blocks=(0, 1, 2, 3)):
                junk = squares[:] if t is not None else tmp2[:].rearrange("p a n -> p (a n)")
                for i in blocks:
                    act.wait_ge(x_loaded[i], 16 * T + 16)
                    square = A(junk, xn[:, i, :], ACT.Square, accum_out=ssq_x[:, i:i + 1])
                    if i == 3:
                        square.then_inc(x_squared, 1)
                    else:
                        link(square, t)

            def h_high(T, k):
                act.wait_ge(xT_plain, T * KB_D + (k + 1))
                A(h_hi[:, k, :], tmp2[:, k % 2, :], ACT.Copy).then_inc(h_hi_ready, 1)

            x_square(0, None)
            for k in range(KB_D):
                h_high(0, k)

            assert steps[0] == ACT_BEFORE, steps
            steps[0] = 0

            with act.Fori(0, TILES) as t:
                for s in range(SLOTS):
                    panel, b = s // 4, s % 4
                    f = first_fill(s)
                    a = acc[f % 2]
                    if panel in (P_QA, P_VB, P_GA, P_GB) + P_ZM or panel == P_KVQ and b >= 2:
                        act.wait_ge(acc_full, filled(t, f))
                    if panel == P_QA:
                        A(qT[:, b, :], a[:], ACT.Copy).then_inc(acc_free[f % 2], 1)
                    if panel == P_KVQ and b >= 2:
                        A(qbT[:, b - 2, :], a[:], ACT.Copy, scale=B_K ** -0.5).then_inc(acc_free[f % 2], 1)
                    if panel == P_VB:
                        A(vb[:, b, :], a[:], ACT.Copy).then_inc(acc_free[f % 2], 1)
                    if panel in (P_GA, P_GB):
                        A(tmp[:, b % 2, :], a[:], ACT.Tanh, scale=0.5).then_inc(gate_tanh, 1)
                    if panel in P_ZM:
                        dst = (gate_a, gate_b)[P_ZM.index(panel) % 2]
                        A(dst[:, b, :], a[:], ACT.Tanh, scale=0.5).then_inc(acc_free[f % 2], 1)
                    if 0 <= s - 8 < 8:
                        u = s - 8
                        act.wait_ge(ptrans_full, t * 8 + (u + 1))
                        A(probsT[:, u % 2, 0, :, :].rearrange("p j q -> p (j q)"), ps_t[:, 0, :], ACT.Copy
                          ).then_inc(ptrans_act, 1)
                    if 0 <= s - 7 < 8:
                        u = s - 7
                        act.wait_ge(negmax, t * 8 + (u + 1))
                        for j in range(A_GROUP):
                            pr = probs[:, u % 2, j, CHUNK:256]
                            A(pr, pr, ACT.Exp, bias=nmax[:, u, j:j + 1], scale=1.0 / SINK_SCALE,
                              accum_out=sums[:, u, j:j + 1])
                        A(esink[:, u, :], esink[:, u, :], ACT.Exp, scale=1.0 / SINK_SCALE).then_inc(probs_ready, 1)
                    if s == 17:
                        act.wait_ge(z_full, t + 1)
                        link(A(lscr[:], ps_s[:], ACT.Abs), t)
                        link(A(lscr[:], lscr[:], ACT.Exp, scale=-1.0), t)
                        A(lscr[:], lscr[:], ACT.Ln, bias=1.0).then_inc(log_ready, 1)
                    if s == 19:
                        act.wait_ge(cum_full, t + 1)
                        A(lscr[:], ps_s[:], ACT.Exp)
                        A(decay, ps_y[:, 0:16], ACT.Exp).then_inc(decay_ready, 1)
                    if 21 <= s < 25:
                        i = s - 21
                        if i:
                            act.wait_ge(o_squared, t * 4 + i)
                        act.wait_ge(o_full, t * 4 + (i + 1))
                        for hd in range(B_HEADS):
                            hp, low = hd // 2, hd % 2
                            last = A(tmp2[:, 0, hd * B_V:(hd + 1) * B_V],
                                     (ps_o, ps_y)[low][:, hp * B_V:(hp + 1) * B_V], ACT.Square,
                                     accum_out=ssq_o[:, i * 4 + hd:i * 4 + hd + 1])
                        last.then_inc(o_squared, 1)
                    if 20 <= s < 24 or 27 <= s < 31:
                        n = s - 20 if s < 24 else s - 23
                        act.wait_ge(yT_full, t * 8 + (n + 1))
                        A(y_hi[:, n, :], ps_t[:, n % 2, :], ACT.Identity, scale=0.5 if n < 4 else half_g
                          ).then_inc(yT_hi_ready, 1)
                    if panel in P_BR:
                        n = 4 * P_BR.index(panel) + b
                        act.wait_ge(m_plain, t * 8 + (n + 1))
                        A(m_hi[:, n, :], tmp[:, b % 2, :], ACT.Copy).then_inc(m_hi_ready, 1)
                    if s == 4 * P_BR[1] + 2:
                        act.wait_ge(m_ready, t * 8 + 6)
                        for i in (0, 2):
                            act.dma_start(xn[:, i, :], x_block((t + 1) % TILES, i)).then_inc(x_loaded[i], 16)
                    if s == 4 * P_BR[1] + 3:
                        act.wait_ge(m_ready, t * 8 + 8)
                        for i in range(TB):
                            act.dma_start(res[:, i, :], x_block(t, i)).then_inc(res_loaded[i], 16)
                        for i in (1, 3):
                            act.dma_start(xn[:, i, :], x_block((t + 1) % TILES, i)).then_inc(x_loaded[i], 16)
                    if s == 48:
                        x_square(t + 1, t, (0, 2))
                    if s == 50:
                        x_square(t + 1, t, (1, 3))
                    if s >= 52:
                        h_high(t + 1, 2 * (s - 52))
                        h_high(t + 1, 2 * (s - 52) + 1)
                        i = s - 52
                        if i == 0:
                            act.wait_ge(x_squared, t + 2)
                        else:
                            act.wait_ge(res_squared, t * 4 + i)
                        act.wait_ge(res_ready, t * 8 + (5 + i))
                        A(squares[:], res[:, i, :], ACT.Square, accum_out=ssq_f[:, i:i + 1]).then_inc(res_squared, 1)
                assert steps[0] == ACT_TILE, steps
                for i in range(TB):
                    act.wait_ge(result_ready, t * 4 + (i + 1))
                    act.dma_start(out[bass.ds(t * NT + i * P, P), :], res[:, i, :]).then_inc(stored, 16)


def shape_constants():
    r = np.arange(P)
    ident = np.eye(P, dtype=np.float32)
    same = r[:, None] // CHUNK == r[None, :] // CHUNK
    suffix = (same & (r[:, None] > r[None, :])).astype(np.float32) / np.float32(16.0)
    chunks = (r[:, None] // CHUNK == np.arange(2)[None, :]).astype(np.float32) / np.float32(16.0)
    key = np.arange(WIN)
    d = np.abs(r[:, None] + CHUNK - key[None, :]).astype(np.float32)
    seen = (key[None, :] // CHUNK == r[:, None] // CHUNK) | (key[None, :] // CHUNK == r[:, None] // CHUNK + 1)
    inner = np.where(seen, d, np.float32(MASKED))
    first = np.where(seen & (key[None, :] >= CHUNK), d, np.float32(MASKED))
    dist = np.ascontiguousarray(np.stack([first, inner], axis=1).astype(np.float32))
    return ident, suffix, chunks, dist


def kernel(x, c, ada_w, ada_b, norm_g, w_in, w_alpha, b_alpha, sinks, head_norm_g,
           w_branch_a, w_branch_b, w_out, final_norm_g):
    from concourse import bacc
    from concourse.bass_utils import run_bass_kernel_spmd

    def columns(a):
        return np.ascontiguousarray(np.asarray(a).reshape(-1, P).T)

    a = {k: np.asarray(v) for k, v in dict(
        x=x, c=c, ada_w=ada_w, ada_b=ada_b, norm_g=norm_g, w_in=w_in, w_alpha=w_alpha, b_alpha=b_alpha, sinks=sinks,
        head_norm_g=head_norm_g, w_branch_a=w_branch_a, w_branch_b=w_branch_b, w_out=w_out,
        final_norm_g=final_norm_g).items()}
    ident, suffix, chunks, dist = shape_constants()
    inputs = [
        ("x", a["x"][0]), ("c", columns(a["c"][0])), ("ada_w", a["ada_w"][0]), ("ada_b", columns(a["ada_b"][0, :2 * D])),
        ("norm_g", columns(a["norm_g"][0])), ("w_in", a["w_in"][0]), ("w_alpha", a["w_alpha"][0]),
        ("b_alpha", a["b_alpha"]), ("sinks", a["sinks"][0]), ("head_g", columns(a["head_norm_g"][0])),
        ("w_br_a", a["w_branch_a"][0]), ("w_br_b", a["w_branch_b"][0]), ("w_out", a["w_out"][0]),
        ("final_g", a["final_norm_g"]), ("ada_b_row", a["ada_b"][0, 2 * D:]),
        ("ident", ident), ("suffix", suffix), ("chunks", chunks), ("dist", dist),
    ]
    nc = bacc.Bacc("TRN2", target_bir_lowering=False, num_devices=1)
    arrays, args = {}, []
    for name, value in inputs:
        value = np.ascontiguousarray(value)
        arrays["in_" + name] = value
        args.append(nc.dram_tensor("in_" + name, value.shape, mybir.dt.from_np(value.dtype), kind="ExternalInput").ap())
    out = nc.dram_tensor("out_0", (SEQ, D), mybir.dt.float32, kind="ExternalOutput").ap()
    build(nc, *args, out)
    r = run_bass_kernel_spmd(nc, [arrays], core_ids=[0])
    return np.asarray(r.results[0]["out_0"]).reshape(1, SEQ, D)
```

```python
import numpy as np
import concourse.bass as bass
from concourse import mybir

P = 128
D = 1024
SEQ = 2048
NT = 512
TILES = SEQ // NT
KB_D = D // P
TB = NT // P
CHUNK = 64
A_HEADS, A_GROUP, A_DIM = 8, 4, 64
WIN = 3 * CHUNK
B_HEADS, B_K, B_V = 4, 64, 128
RANK = 16
EPS = 1e-6
MASKED = 1e33
SINK_SCALE = 8.0
RSQRT_MAGIC = 0x5F3759DF

QA, KA, VA, GA, QB, KB, VB, GB, ZA, ZM = 0, 512, 640, 768, 1280, 1536, 1792, 2304, 2816, 2832
PANELS = [
    ("w_in", [(QA, 512)]),
    ("w_in", [(KA, 256), (QB, 256)]),
    ("w_in", [(GA, 512)]),
    ("w_in", [(KB, 256), (ZA, RANK)]),
    ("w_in", [(VB, 512)]),
    ("w_in", [(GB, 512)]),
    ("w_in", [(ZM, 512)]),
    ("w_in", [(ZM + D, 512)]),
    ("w_br", [(0, 512)]),
    ("w_in", [(ZM + 512, 512)]),
    ("w_in", [(ZM + D + 512, 512)]),
    ("w_br", [(512, 512)]),
    ("w_out", [(0, 512)]),
    ("w_out", [(512, 512)]),
]
P_QA, P_KVQ, P_GA, P_KZ, P_VB, P_GB = range(6)
P_ZM = (6, 7, 9, 10)
P_BR = (8, 11)
P_OUT = (12, 13)
SLOTS = 4 * len(PANELS)
DUOS = 4 * len(PANELS)
RING = 7
STAGES = 2
WIDTH = [sum(n for _, n in cols) for _, cols in PANELS]
FILLS = SLOTS + 8
MOD_GROUPS = [(0, D), (D, D + 512), (D + 512, 2 * D)]


def first_fill(slot):
    return slot + sum(min(max(slot - 4 * p, 0), 4) for p in P_BR)


def build(nc, x, c, ada_w, ada_b, norm_g, w_in, w_alpha, b_alpha, sinks, head_g, w_br_a, w_br_b, w_out,
          final_g, ada_b_row, ident_in, suffix_in, chunks_in, dist_in, out):
    F32, F32R, I32 = mybir.dt.float32, mybir.dt.float32r, mybir.dt.int32
    ACT, ALU, AX = mybir.ActivationFunctionType, mybir.AluOpType, mybir.AxisListType
    KIB = 1024

    cursor = [(nc.sbuf_base + 63) // 64 * 64]

    def place(name, shape, dt=F32, at=None):
        size = 4 * int(np.prod(shape[1:]))
        offset = cursor[0] if at is None else at
        if at is None:
            cursor[0] += (size + 31) // 32 * 32
        return nc.alloc_sbuf_tensor_at(name, shape, dt, offset=offset)

    def region(kib):
        at = cursor[0]
        cursor[0] += kib * KIB
        return at

    r_h, r_y, r_qv, r_hi, r_lo = region(32), region(32), region(16), region(16), region(16)
    h_hi = place("h_hi", [P, KB_D, NT], F32R, at=r_h)
    h_lo = place("h_lo", [P, KB_D, NT], F32R, at=r_h + 16 * KIB)
    y_hi = place("y_hi", [P, 8, NT], F32R, at=r_y)
    y_lo = place("y_lo", [P, 8, NT], F32R, at=r_y + 16 * KIB)
    probs = place("probs", [P, 2, A_GROUP, 256], at=r_y + 8 * KIB)
    probsT = place("probsT", [P, 2, 2, A_GROUP, P], at=r_y + 24 * KIB)
    res = place("res", [P, TB, D], at=r_y)
    squares = place("squares", [P, D], at=r_y + 16 * KIB)
    qT = place("qT", [P, 4, NT], at=r_qv)
    vb = place("vb", [P, TB, 512], at=r_qv + 8 * KIB)
    gate_a = place("gate_a", [P, 4, NT], at=r_qv)
    gate_b = place("gate_b", [P, 4, NT], at=r_qv + 8 * KIB)
    xn = place("xn", [P, TB, D], at=r_qv)
    ya = place("ya", [P, TB, 512], at=r_hi)
    yb = place("yb", [P, TB, 512], at=r_hi + 8 * KIB)
    m_hi = place("m_hi", [P, KB_D, NT], F32R, at=r_hi)
    qbT = place("qbT", [P, 2, NT], at=r_lo)
    kb = place("kb", [P, TB, 256], at=r_lo + 4 * KIB)
    la = place("la", [P, TB, 256], at=r_lo + 8 * KIB)
    lscr = place("lscr", [P, TB, 256], at=r_lo + 12 * KIB)
    m_lo = place("m_lo", [P, KB_D, NT], F32R, at=r_lo)
    ada_ss = [place(f"ada_ss{k}", [P, 2 * D], at=(r_y if k < 4 else r_h) + 8 * KIB * (k % 4)) for k in range(KB_D)]
    ada_gt = [place(f"ada_gt{k}", [P, D], at=r_hi + 4 * KIB * k) for k in range(KB_D)]

    w_split = place("w_split_hi", [P, RING, 2, 512], F32R)
    w_split_lo = place("w_split_lo", [P, RING, 2, 512], F32R)
    stage = [place(f"stage{i}", [P, 2, 512]) for i in range(STAGES)]
    kT = place("kT", [P, CHUNK + NT])
    v = place("v", [P, 1 + TB, P])
    state = place("state", [P, 4, 256])
    dist = place("dist", [P, 2, WIN])
    ident = place("ident", [P, P])
    suffix = place("suffix", [P, P])
    chunks = place("chunks", [P, 2])
    gate_row = place("gate_row", [P, D])
    final_row = place("final_row", [P, D])
    w_al = place("w_al", [RANK + 1, 256])
    zaT = place("zaT", [RANK + 1, NT])
    za = place("za", [P, TB, RANK])
    ones = place("ones", [P, P], at=r_y + 8 * KIB)
    tmp = place("tmp", [P, 2, 512])
    tmp2 = place("tmp2", [P, 2, 512])
    small = place("small", [P, 336])
    h_plain = [tmp2[:, 0, :], tmp2[:, 1, :], tmp[:, 0, :], tmp[:, 1, :]]
    assert cursor[0] <= nc.sbuf_usable_end, cursor[0]

    used = [0]

    def cell(n):
        a = used[0]
        used[0] += n
        return small[:, a:a + n]

    c_col, c_tanh, c_silu = cell(8), cell(8), cell(8)
    shift, gscale, modb, norm_col = cell(8), cell(8), cell(16), cell(8)
    half_g, sink8, ones_col = cell(1), cell(8), cell(1)
    maxs, nmax, esink, sums, rden = (cell(32).rearrange("p (u j) -> p u j", j=4) for _ in range(5))
    decay = cell(16)
    ssq_x, ssq_o, ssq_f = cell(4), cell(16), cell(4)
    rs_x, rs_o, rs_f = cell(4), cell(16), cell(4)
    rs_m, rs_t = cell(16), cell(16)
    assert used[0] <= 336, used

    def psum(name, shape):
        return nc.alloc_psum_tensor(name, shape, F32)

    acc = [psum(f"acc{i}", [P, 512]) for i in range(2)]
    ps_s = psum("ps_s", [P, 4, 256])
    ps_t = psum("ps_t", [P, 2, 512])
    ps_y = psum("ps_y", [P, 512])
    ps_o = psum("ps_o", [P, 512])

    first_banks = [ps_t[:, 0, :], ps_t[:, 1, :], ps_s[:, 0:2, :].rearrange("p a n -> p (a n)"),
                   ps_s[:, 2:4, :].rearrange("p a n -> p (a n)"), ps_y[:], ps_o[:], ps_t[:, 0, :], ps_t[:, 1, :]]

    names = """consts_loaded c_loaded stored
        w_ready w_used acc_full
        c_tanh_done ss_summed gt_summed mod_full gscale_ready gate_full gate_ready
        x_squared x_scaled xT_full h_hi_ready h_ready
        gate_tanh vT_full v_ready
        scores_full scores_read negmax probs_ready ptrans_full ptrans_act ptrans_dve pv_full y_scaled
        zaT_full zaT_ready z_full log_ready la_ready cum_full decay_ready kb_ready kv_full state_ready
        o_full o_squared o_gated yb_ready yT_full yT_hi_ready yT_ready
        m_plain m_hi_ready m_ready res_ready res_squared result_ready
        dve_step act_step pool_step pe_turn pool_turn""".split()
    S = {n: nc.alloc_semaphore(n) for n in names}
    acc_free = [nc.alloc_semaphore(f"acc_free{i}") for i in range(2)]
    xT_read = [nc.alloc_semaphore(f"xT_read{i}") for i in range(2)]
    x_loaded = [nc.alloc_semaphore(f"x_loaded{i}") for i in range(TB)]
    res_loaded = [nc.alloc_semaphore(f"res_loaded{i}") for i in range(TB)]
    ss_loaded = [[nc.alloc_semaphore(f"ss_loaded{n}_{k}") for k in range(KB_D)] for n in range(len(MOD_GROUPS))]
    gt_loaded = [nc.alloc_semaphore(f"gt_loaded{k}") for k in range(KB_D)]
    stage_loaded = [nc.alloc_semaphore(f"stage_loaded{i}") for i in range(STAGES)]
    (consts_loaded, c_loaded, stored,
     w_ready, w_used, acc_full,
     c_tanh_done, ss_summed, gt_summed, mod_full, gscale_ready, gate_full, gate_ready,
     x_squared, x_scaled, xT_full, h_hi_ready, h_ready,
     gate_tanh, vT_full, v_ready,
     scores_full, scores_read, negmax, probs_ready, ptrans_full, ptrans_act, ptrans_dve, pv_full, y_scaled,
     zaT_full, zaT_ready, z_full, log_ready, la_ready, cum_full, decay_ready, kb_ready, kv_full, state_ready,
     o_full, o_squared, o_gated, yb_ready, yT_full, yT_hi_ready, yT_ready,
     m_plain, m_hi_ready, m_ready, res_ready, res_squared, result_ready,
     dve_step, act_step, pool_step, pe_turn, pool_turn) = (S[n] for n in names)

    CONSTS = 12
    def may_fill(t, f):
        return t * (FILLS // 2) + (f // 2 + 1)

    def filled(t, f):
        return t * FILLS + (f + 1)

    def w_src(panel, duo):
        matrix = PANELS[panel][0]
        if matrix == "w_br":
            return (w_br_a if duo < 2 else w_br_b), 2 * P * (duo % 2)
        return (w_in if matrix == "w_in" else w_out), 2 * P * duo

    loads_of = [len(PANELS[d // 4][1]) for d in range(DUOS)]
    loads_upto = [sum(n for e, n in enumerate(loads_of[:d + 1]) if e % STAGES == d % STAGES) for d in range(DUOS)]
    loads_tile = [sum(n for e, n in enumerate(loads_of) if e % STAGES == i) for i in range(STAGES)]

    def x_block(t, i):
        return x[bass.ds(t * NT + i * P, P), :]

    block = nc.Block()
    with block:
        @block.sync
        def _(sp):
            sp.dma_start(c_col, c).then_inc(c_loaded, 16)
            for i in range(TB):
                sp.dma_start(xn[:, i, :], x[i * P:(i + 1) * P, :]).then_inc(x_loaded[i], 16)

            def load_duo(d):
                src, row = w_src(d // 4, d % 4)
                col = 0
                for first, n in PANELS[d // 4][1]:
                    sp.dma_start(stage[d % STAGES][:, :, col:col + n],
                                 src[row:row + 2 * P, first:first + n].rearrange("(k p) n -> p k n", p=P)
                                 ).then_inc(stage_loaded[d % STAGES], 16)
                    col += n

            for d in range(STAGES):
                load_duo(d)
            for n, (m0, m1) in enumerate(MOD_GROUPS):
                for k in range(KB_D):
                    sp.dma_start(ada_ss[k][:, m0:m1], ada_w[k * P:(k + 1) * P, m0:m1]).then_inc(ss_loaded[n][k], 16)
            with sp.Fori(0, TILES) as t:
                for d in range(STAGES, DUOS + STAGES):
                    sp.wait_ge(w_ready, t * DUOS + (d - STAGES + 1))
                    load_duo(d % DUOS)
            for xl in x_loaded:
                sp.wait_ge(xl, 16 * (TILES + 1))
            for i in range(STAGES):
                sp.wait_ge(stage_loaded[i], TILES * (16 * loads_tile[i]) + 16 * loads_upto[i])
            sp.wait_ge(stored, 16 + 16 * TB * TILES)

        @block.gpsimd
        def _(pool):
            with pool.Fori(0, TILES) as t:
                for d in range(DUOS):
                    n, r, s = WIDTH[d // 4], d % RING, d % STAGES
                    pool.wait_ge(stage_loaded[s], t * (16 * loads_tile[s]) + 16 * loads_upto[d])
                    pool.wait_ge(w_used, t * DUOS + (d + 1))
                    pool.sem_inc(pool_turn, 1)
                    if d // 4 == P_QA:
                        def split_as(z, k):
                            return z[:, r, k, :].rearrange("p (j g e) -> p j g e", g=2, j=4)
                        parts = [(split_as(w_split, k), split_as(w_split_lo, k),
                                  stage[s][:, k, :].rearrange("p (g j e) -> p j g e", g=2, j=4)) for k in range(2)]
                    else:
                        parts = [(w_split[:, r, :, :n], w_split_lo[:, r, :, :n], stage[s][:, :, :n])]
                    for hi, _, raw in parts:
                        last = nc.gpsimd.tensor_scalar(hi, raw, 1.0, 1.0, ALU.mult, ALU.mult)
                    last.then_inc(pool_step, 1)
                    pool.wait_ge(pool_step, t * DUOS + (d + 1))
                    for hi, lo, raw in parts:
                        last = nc.gpsimd.tensor_tensor(lo, raw, hi.bitcast(F32), ALU.subtract)
                    last.then_inc(w_ready, 1)

        @block.tensor
        def _(pe):
            mm = nc.tensor.matmul

            def x_transpose(bank, T, k):
                for i in range(TB):
                    last = nc.tensor.transpose(bank[:, i * P:(i + 1) * P], xn[:, i, k * P:(k + 1) * P], ident[:])
                last.then_inc(xT_full, 1)

            pe.sem_inc(w_used, RING - 1)
            pe.wait_ge(consts_loaded, 16 * CONSTS)
            pe.wait_ge(x_scaled, 1)
            for k in range(6):
                x_transpose(first_banks[k], 0, k)
            for n, (m0, m1) in enumerate(MOD_GROUPS):
                pe.wait_ge(ss_summed, n + 1)
                for j in range(m0 // P, m1 // P):
                    last = mm(acc[n // 2][:, j:j + 1], ada_ss[0][:, j * P:(j + 1) * P], ones_col,
                              start=True, stop=True)
                last.then_inc(mod_full, 1)
            for k in (6, 7):
                pe.wait_ge(xT_read[k % 2], 1)
                x_transpose(first_banks[k], 0, k)

            with pe.Fori(0, TILES) as t:
                def three(o, a_hi, a_lo, b_hi, b_lo, start, stop):
                    first = mm(o, a_hi, b_hi, start=start, stop=False)
                    mm(o, a_hi, b_lo, start=False, stop=False)
                    return first, mm(o, a_lo, b_hi, start=False, stop=stop)

                def weights(panel, k, cols):
                    r = (4 * panel + k // 2) % RING
                    return w_split[:, r, k % 2, cols], w_split_lo[:, r, k % 2, cols]

                def fill(f, panel, ks, first, last_fill, step, ready=None):
                    pe.wait_ge(acc_free[f % 2], may_fill(t, f))
                    for k in ks:
                        duo = 4 * panel + k // 2
                        if first and k % 2 == 0:
                            pe.wait_ge(w_ready, t * DUOS + (duo + 1))
                        if ready is not None and k == ks[0] or ready is not None and ready[2]:
                            pe.wait_ge(ready[0], t * 8 + ready[1](k))
                        product, last = step(k, k == ks[0], k == ks[-1])
                        if first and k == 0:
                            product.then_inc(w_used, 1)
                        if last_fill and k % 2 and k != ks[-1]:
                            last.then_inc(w_used, 1)
                        if last_fill and k == 4 and ks[0] == 4:
                            product.then_inc(w_used, 1)
                    last.then_inc(acc_full, 1)

                def transposed(panel, f, c0, b, ks, first, last_fill, ready=None):
                    b_hi, b_lo = b

                    def step(k, start, stop):
                        w_hi, w_lo = weights(panel, k, slice(c0, c0 + P))
                        return three(acc[f % 2][:], w_hi, w_lo, b_hi[:, k, :], b_lo[:, k, :], start, stop)

                    fill(f, panel, ks, first, last_fill, step, ready)

                def by_token(panel, f, i, n, a, first, last_fill, ready=None):
                    a_hi, a_lo = a
                    tok = slice(i * P, (i + 1) * P)

                    def step(k, start, stop):
                        w_hi, w_lo = weights(panel, k, slice(0, n))
                        return three(acc[f % 2][:, :n], a_hi[:, k, tok], a_lo[:, k, tok], w_hi, w_lo, start, stop)

                    fill(f, panel, ks_all, first, last_fill, step, ready)

                def evacuated(f):
                    pe.wait_ge(acc_free[f % 2], may_fill(t, f) + 1)

                ks_all = list(range(KB_D))
                h = (h_hi, h_lo)

                def dense(s):
                    panel, b = s // 4, s % 4
                    f = first_fill(s)
                    first, last_fill = b == 0, b == 3
                    if panel == P_QA:
                        transposed(panel, f, b * P, h, ks_all, first, last_fill,
                                   ready=(h_ready, lambda k: k + 1, True) if first else None)
                    elif panel == P_KVQ:
                        transposed(panel, f, b * P, h, ks_all, first, last_fill)
                    elif panel in (P_GA, P_KZ, P_VB, P_GB):
                        by_token(panel, f, b, WIDTH[panel], h, first, last_fill)
                    elif panel in P_ZM:
                        transposed(panel, f, b * P, h, ks_all, first, last_fill)
                    elif panel in P_BR:
                        y = (y_hi, y_lo)
                        pair = P_BR.index(panel) == 0 and first
                        transposed(panel, f, b * P, y, ks_all[:4], first, last_fill,
                                   ready=(yT_ready, lambda k: 4, False) if pair else None)
                        transposed(panel, f + 1, b * P, y, ks_all[4:], first, last_fill,
                                   ready=(yT_ready, lambda k: 8, False) if pair else None)
                    else:
                        by_token(panel, f, b, 512, (m_hi, m_lo), first, last_fill,
                                 ready=(m_ready, lambda k: k + 1, True) if panel == P_OUT[0] and first else None)

                def scores(u):
                    pair, g = u // 2, u % 2
                    if u == 0:
                        pe.wait_ge(gate_ready, 1)
                        evacuated(3)
                        evacuated(first_fill(4 * P_KVQ))
                    else:
                        pe.wait_ge(scores_read, t * 8 + u)
                    rows = slice(g * A_DIM, (g + 1) * A_DIM)
                    for j in range(A_GROUP):
                        last = mm(ps_s[:, j, 0:WIN], qT[rows, j, pair * P:(pair + 1) * P],
                                  kT[rows, pair * P:pair * P + WIN], start=True, stop=True)
                    last.then_inc(scores_full, 1)

                def adaln_gate():
                    pe.wait_ge(gt_summed, 1)
                    for half in range(2):
                        last = mm(ps_s[:, 2 * half:2 * half + 2, :], ones[:], ada_gt[0][:, half * 512:half * 512 + 512],
                                  start=True, stop=True)
                    last.then_inc(gate_full, 1)

                def v_transpose():
                    evacuated(first_fill(4 * P_KVQ + 1))
                    for i in range(TB):
                        last = nc.tensor.transpose(ps_t[:, 0, i * P:(i + 1) * P], tmp2[:, 0, i * P:(i + 1) * P], ident[:])
                    last.then_inc(vT_full, 1)

                def transpose_probs(u):
                    pe.wait_ge(probs_ready, t * 8 + (u + 1))
                    if u == 0:
                        pe.wait_ge(v_ready, t + 1)
                    if u:
                        pe.wait_ge(ptrans_act, t * 8 + u)
                        pe.wait_ge(ptrans_dve, t * 8 + u)
                    for half, c0 in ((0, P), (1, 0)):
                        for j in range(A_GROUP):
                            last = nc.tensor.transpose(ps_t[:, half, j * P:(j + 1) * P],
                                                       probs[:, u % 2, j, c0:c0 + P], ident[:])
                    last.then_inc(ptrans_full, 1)

                def attend(u):
                    pair, g = u // 2, u % 2
                    if u == 0:
                        pe.wait_ge(v_ready, t + 1)
                    else:
                        pe.wait_ge(y_scaled, t * 8 + u)
                    pe.wait_ge(ptrans_act, t * 8 + (u + 1))
                    pe.wait_ge(ptrans_dve, t * 8 + (u + 1))
                    vc = slice(g * A_DIM, (g + 1) * A_DIM)
                    for j in range(A_GROUP):
                        o = ps_y[:, j * A_DIM:(j + 1) * A_DIM]
                        mm(o, probsT[:, u % 2, 0, j, :], v[:, pair + 1, vc], start=True, stop=False)
                        last = mm(o, probsT[CHUNK:P, u % 2, 1, j, :], v[CHUNK:P, pair, vc], start=False, stop=True)
                    last.then_inc(pv_full, 1)

                def y_transpose(n):
                    if n == 0:
                        pe.wait_ge(y_scaled, t * 8 + 8)
                    if n == 4:
                        pe.wait_ge(yb_ready, t + 1)
                    if n >= 2:
                        pe.wait_ge(yT_ready, t * 8 + (n - 1))
                    src = ya if n < 4 else yb
                    for i in range(TB):
                        last = nc.tensor.transpose(ps_t[:, n % 2, i * P:(i + 1) * P],
                                                   src[:, i, (n % 4) * P:(n % 4 + 1) * P], ident[:])
                    last.then_inc(yT_full, 1)

                def za_transpose():
                    evacuated(first_fill(4 * P_KZ + 2))
                    evacuated(first_fill(4 * P_KZ + 3))
                    for i in range(TB):
                        last = nc.tensor.transpose(ps_t[0:RANK, 0, i * P:(i + 1) * P], za[:, i, :], ident[:])
                    last.then_inc(zaT_full, 1)

                def decay_logits():
                    pe.wait_ge(zaT_ready, t + 1)
                    pe.wait_ge(scores_read, t * 8 + 8)
                    for i in range(TB):
                        last = mm(ps_s[:, i, :], zaT[:, i * P:(i + 1) * P], w_al[:], start=True, stop=True)
                    last.then_inc(z_full, 1)

                def suffix_sums():
                    pe.wait_ge(la_ready, t + 1)
                    pe.wait_ge(y_scaled, t * 8 + 8)
                    for i in range(TB):
                        mm(ps_s[:, i, :], suffix[:], la[:, i, :], start=True, stop=True)
                    for i in range(TB):
                        for hp in range(2):
                            a = hp * 8 + 2 * i
                            last = mm(ps_y[:, a:a + 2], la[:, i, hp * P:(hp + 1) * P], chunks[:], start=True, stop=True)
                    last.then_inc(cum_full, 1)

                def key_values(i):
                    if i == 0:
                        pe.wait_ge(kb_ready, t + 1)
                        evacuated(first_fill(4 * P_VB + 2))
                        evacuated(first_fill(4 * P_VB + 3))
                    else:
                        pe.wait_ge(state_ready, t * 4 + i)
                    pe.sem_inc(pe_turn, 1)
                    for c2 in range(2):
                        rows = slice(c2 * CHUNK, (c2 + 1) * CHUNK)
                        for hd in range(B_HEADS):
                            hp, low = hd // 2, hd % 2
                            last = mm(ps_s[low * B_K:(low + 1) * B_K, 2 * c2, hp * P:(hp + 1) * P], kb[rows, i, hd * B_K:(hd + 1) * B_K],
                                      vb[rows, i, hd * B_V:(hd + 1) * B_V], start=True, stop=True)
                    last.then_inc(kv_full, 1)

                def read_state(i):
                    pe.wait_ge(state_ready, t * 4 + (i + 1))
                    if i == 0:
                        evacuated(first_fill(4 * P_KVQ + 2))
                        evacuated(first_fill(4 * P_KVQ + 3))
                    else:
                        pe.wait_ge(o_gated, t * 4 + i)
                    pe.sem_inc(pe_turn, 1)
                    for c2 in range(2):
                        tok = slice(i * P + c2 * CHUNK, i * P + (c2 + 1) * CHUNK)
                        for hd in range(B_HEADS):
                            hp, low = hd // 2, hd % 2
                            rows = slice(low * B_K, (low + 1) * B_K)
                            last = mm((ps_o, ps_y)[low][c2 * CHUNK:(c2 + 1) * CHUNK, hp * B_V:(hp + 1) * B_V],
                                      qbT[rows, hp, tok], state[rows, (2 * i + c2) % 4, hp * P:(hp + 1) * P],
                                      start=True, stop=True)
                    last.then_inc(o_full, 1)

                for s in range(SLOTS):
                    dense(s)
                    if 0 <= s - 7 < 8:
                        scores(s - 7)
                    if 0 <= s - 9 < 8:
                        attend(s - 9)
                    if 0 <= s - 8 < 8:
                        transpose_probs(s - 8)
                    if s == 4:
                        with pe.If(t == 0):
                            adaln_gate()
                    if s == 6:
                        v_transpose()
                    if s == 16:
                        za_transpose()
                    if s == 17:
                        decay_logits()
                    if s == 19:
                        suffix_sums()
                    if 20 <= s < 24:
                        y_transpose(s - 20)
                        key_values(s - 20)
                    if 21 <= s < 25:
                        read_state(s - 21)
                    if 27 <= s < 31:
                        y_transpose(s - 23)
                    if 51 <= s < 55:
                        for k in (2 * (s - 51), 2 * (s - 51) + 1):
                            if k == 0:
                                pe.wait_ge(x_scaled, (t + 1) + 1)
                            if k >= 2:
                                pe.wait_ge(xT_read[k % 2], (t + 1) * 4 + k // 2)
                            x_transpose(ps_t[:, k % 2, :], t + 1, k)

        @block.vector
        def _(dve):
            V = nc.vector
            steps = [0]
            DVE_BEFORE, DVE_TILE = 46, 86

            def link(ins, t=None):
                ins.then_inc(dve_step, 1)
                steps[0] += 1
                if t is None:
                    dve.wait_ge(dve_step, steps[0])
                else:
                    dve.wait_ge(dve_step, t * DVE_TILE + (DVE_BEFORE + steps[0]))

            def rsqrt(out_, sq, n, count, t):
                m, a = rs_m[:, :count], rs_t[:, :count]
                link(V.tensor_scalar(m, sq, 1.0 / n, EPS, ALU.mult, ALU.add), t)
                V.tensor_scalar(out_.bitcast(I32), m.bitcast(I32), -0.5, float(RSQRT_MAGIC), ALU.mult, ALU.add)
                link(V.tensor_scalar(a, m, -0.5, None, ALU.mult), t)
                for _ in range(3):
                    if count == 1:
                        link(V.scalar_tensor_tensor(m, out_, a, out_, ALU.mult, ALU.mult), t)
                    else:
                        link(V.tensor_tensor(m, out_, out_, ALU.mult), t)
                        link(V.tensor_tensor(m, m, a, ALU.mult), t)
                    link(V.scalar_tensor_tensor(out_, m, 1.5, out_, ALU.add, ALU.mult), t)

            def x_scale(T, t):
                dve.wait_ge(x_squared, T + 1)
                rsqrt(rs_x, ssq_x, D, TB, t)
                for i in range(TB):
                    last = V.tensor_scalar(xn[:, i, :], xn[:, i, :], rs_x[:, i:i + 1], None, ALU.mult)
                last.then_inc(x_scaled, 1)

            def affine(T, k, bank, buf):
                dve.wait_ge(xT_full, T * KB_D + (k + 1))
                V.tensor_scalar(buf, bank, gscale[:, k:k + 1], shift[:, k:k + 1], ALU.mult, ALU.add
                                ).then_inc(xT_read[0], 1)

            def h_low(T, k, buf):
                dve.wait_ge(h_hi_ready, T * KB_D + (k + 1))
                V.tensor_tensor(h_lo[:, k, :], buf, h_hi[:, k, :].bitcast(F32), ALU.subtract).then_inc(h_ready, 1)

            V.memset(kT[:, 0:CHUNK], 0.0)
            V.memset(v[:, 0, :], 0.0)
            V.memset(state[:, 3, :], 0.0)
            V.memset(zaT[:], 1.0)
            dve.wait_ge(c_tanh_done, 1)
            link(V.scalar_tensor_tensor(c_silu, c_tanh, 1.0, c_col, ALU.add, ALU.mult))
            link(V.tensor_scalar(c_silu, c_silu, 0.5, None, ALU.mult))
            V.memset(ones_col, 1.0)
            x_scale(0, None)

            def weigh(parts, cols, loaded):
                for k in range(KB_D):
                    dve.wait_ge(loaded[k], 16)
                    part, total = parts[k][:, cols], parts[0][:, cols]
                    if k == 0:
                        link(V.tensor_scalar(total, part, c_silu[:, 0:1], None, ALU.mult))
                    elif k < KB_D - 1:
                        link(V.scalar_tensor_tensor(total, part, c_silu[:, k:k + 1], total, ALU.mult, ALU.add))
                    else:
                        last = V.scalar_tensor_tensor(total, part, c_silu[:, k:k + 1], total, ALU.mult, ALU.add)
                return last

            for n, (m0, m1) in enumerate(MOD_GROUPS):
                weigh(ada_ss, slice(m0, m1), ss_loaded[n]).then_inc(ss_summed, 1)

            def finish_scale(n, k0):
                four = slice(k0, k0 + 4)
                link(V.tensor_tensor(gscale[:, four], acc[n][:, 8 + k0:12 + k0], modb[:, 8 + k0:12 + k0], ALU.add))
                V.scalar_tensor_tensor(gscale[:, four], gscale[:, four], 1.0, norm_col[:, four], ALU.add, ALU.mult
                                       ).then_inc(gscale_ready, 1)
                dve.wait_ge(gscale_ready, n + 1)
                dve.sem_inc(acc_free[n], 1)

            dve.wait_ge(consts_loaded, 16 * CONSTS)
            dve.wait_ge(mod_full, 2)
            V.tensor_tensor(shift, acc[0][:, 0:8], modb[:, 0:8], ALU.add)
            finish_scale(0, 0)
            affine(0, 0, first_banks[0], h_plain[0])
            affine(0, 2, first_banks[2], h_plain[2])
            h_low(0, 0, h_plain[0])
            h_low(0, 1, h_plain[1])
            dve.wait_ge(mod_full, 3)
            finish_scale(1, 4)
            dve.wait_ge(h_ready, 1)
            affine(0, 4, first_banks[4], h_plain[0])
            h_low(0, 2, h_plain[2])
            h_low(0, 3, h_plain[3])
            dve.wait_ge(h_ready, 3)
            affine(0, 6, first_banks[6], h_plain[2])
            for k in range(4, KB_D):
                h_low(0, k, h_plain[k % 4])
            link(V.tensor_scalar(sink8, sink8, SINK_SCALE, None, ALU.mult))
            link(V.tensor_scalar(half_g, half_g, 0.5, None, ALU.mult))
            dve.wait_ge(ss_summed, 3)
            V.memset(ones[:], 1.0)
            weigh(ada_gt, slice(0, D), gt_loaded).then_inc(gt_summed, 1)
            dve.wait_ge(gate_full, 1)
            V.tensor_tensor(gate_row[:], gate_row[:], ps_s[:].rearrange("p a n -> p (a n)"), ALU.add
                            ).then_inc(gate_ready, 1)
            dve.wait_ge(gate_ready, 1)
            link(V.tensor_scalar(gate_row[:], gate_row[:], 0.5, None, ALU.mult))
            assert steps[0] == DVE_BEFORE, steps
            steps[0] = 0

            with dve.Fori(0, TILES) as t:
                def freed(f):
                    dve.wait_ge(acc_free[f % 2], may_fill(t, f) + 1)

                def gate(f, b, out_):
                    dve.wait_ge(gate_tanh, t * 8 + (b + 1))
                    V.scalar_tensor_tensor(out_, tmp[:, b % 2, :], 1.0, acc[f % 2][:], ALU.add, ALU.mult
                                           ).then_inc(acc_free[f % 2], 1)

                def bias_and_max(u):
                    pair, g, b = u // 2, u % 2, u % 2
                    dve.wait_ge(scores_full, t * 8 + (u + 1))
                    for j in range(A_GROUP):
                        slope = 2.0 ** -(A_GROUP * g + j + 1)
                        last = V.scalar_tensor_tensor(probs[:, b, j, CHUNK:256], dist[:, 1 if pair else 0, :],
                                                      -SINK_SCALE * slope, ps_s[:, j, 0:WIN], ALU.mult, ALU.add)
                    last.then_inc(scores_read, 1)
                    dve.wait_ge(scores_read, t * 8 + (u + 1))
                    link(V.tensor_reduce(out=maxs[:, u, :], in_=probs[:, b, :, CHUNK:256], op=ALU.max, axis=AX.X), t)
                    link(V.tensor_tensor(maxs[:, u, :], maxs[:, u, :], sink8[:, 4 * g:4 * g + 4], ALU.max), t)
                    V.tensor_tensor(esink[:, u, :], sink8[:, 4 * g:4 * g + 4], maxs[:, u, :], ALU.subtract)
                    V.tensor_scalar(nmax[:, u, :], maxs[:, u, :], -1.0 / SINK_SCALE, None, ALU.mult).then_inc(negmax, 1)

                def denominators(u):
                    dve.wait_ge(probs_ready, t * 8 + (u + 1))
                    link(V.tensor_tensor(sums[:, u, :], sums[:, u, :], esink[:, u, :], ALU.add), t)
                    link(V.reciprocal(rden[:, u, :], sums[:, u, :]), t)
                    dve.wait_ge(ptrans_full, t * 8 + (u + 1))
                    V.tensor_copy(probsT[CHUNK:P, u % 2, 1, :, :].rearrange("p j q -> p (j q)"),
                                  ps_t[CHUNK:P, 1, :]).then_inc(ptrans_dve, 1)

                def scale_and_gate(u):
                    pair, g = u // 2, u % 2
                    if g == 0:
                        freed(first_fill(4 * P_GA + pair))
                    dve.wait_ge(pv_full, t * 8 + (u + 1))
                    for j in range(A_GROUP):
                        cols = slice((A_GROUP * g + j) * A_DIM, (A_GROUP * g + j + 1) * A_DIM)
                        last = V.scalar_tensor_tensor(ya[:, pair, cols], ps_y[:, j * A_DIM:(j + 1) * A_DIM],
                                                      rden[:, u, j:j + 1], ya[:, pair, cols], ALU.mult, ALU.mult)
                    last.then_inc(y_scaled, 1)

                def y_low(n):
                    dve.wait_ge(yT_hi_ready, t * 8 + (n + 1))
                    V.scalar_tensor_tensor(y_lo[:, n, :], ps_t[:, n % 2, :], 0.5 if n < 4 else half_g,
                                           y_hi[:, n, :].bitcast(F32), ALU.mult, ALU.subtract).then_inc(yT_ready, 1)

                def update_state(i):
                    dve.wait_ge(kv_full, t * 4 + (i + 1))
                    for c2 in range(2):
                        ch = 2 * i + c2
                        for hp in range(2):
                            cols = slice(hp * P, (hp + 1) * P)
                            last = V.scalar_tensor_tensor(state[:, ch % 4, cols], state[:, (ch - 1) % 4, cols],
                                                          decay[:, hp * 8 + ch:hp * 8 + ch + 1],
                                                          ps_s[:, 2 * c2, cols],
                                                          ALU.mult, ALU.add)
                        if c2 == 0:
                            link(last, t)
                    last.then_inc(state_ready, 1)
                    dve.wait_ge(state_ready, t * 4 + (i + 1))

                def normalise(blocks):
                    i0, n = blocks[0], len(blocks)
                    dve.wait_ge(res_squared, t * 4 + (i0 + n))
                    rsqrt(rs_f[:, i0:i0 + n], ssq_f[:, i0:i0 + n], D, n, t)
                    for i in blocks:
                        V.scalar_tensor_tensor(res[:, i, :], res[:, i, :], rs_f[:, i:i + 1], final_row[:],
                                               ALU.mult, ALU.mult).then_inc(result_ready, 1)

                def merge(s, q, j):
                    f, n = first_fill(s), 4 * q + j
                    if j == 0:
                        freed(first_fill(4 * P_ZM[2 * q + 1] + 2))
                        freed(first_fill(4 * P_ZM[2 * q + 1] + 3))
                    if n >= 2:
                        dve.wait_ge(m_ready, t * 8 + (n - 1))
                    dve.wait_ge(acc_full, filled(t, f))
                    V.scalar_tensor_tensor(tmp[:, j % 2, :], gate_a[:, j, :], 1.0, acc[f % 2][:], ALU.add, ALU.mult
                                           ).then_inc(acc_free[f % 2], 1)
                    dve.wait_ge(acc_full, filled(t, f + 1))
                    V.scalar_tensor_tensor(tmp2[:, j % 2, :], gate_b[:, j, :], 1.0, acc[(f + 1) % 2][:], ALU.add, ALU.mult
                                           ).then_inc(acc_free[(f + 1) % 2], 1)
                    freed(f)
                    freed(f + 1)
                    V.tensor_tensor(tmp[:, j % 2, :], tmp[:, j % 2, :], tmp2[:, j % 2, :], ALU.add).then_inc(m_plain, 1)
                    dve.wait_ge(m_hi_ready, t * 8 + (n + 1))
                    V.tensor_tensor(m_lo[:, n, :], tmp[:, j % 2, :], m_hi[:, n, :].bitcast(F32), ALU.subtract
                                    ).then_inc(m_ready, 1)

                for s in range(SLOTS):
                    panel, b = s // 4, s % 4
                    f = first_fill(s)
                    a = acc[f % 2]
                    if panel == P_KVQ and b < 2 or panel == P_KZ:
                        dve.wait_ge(acc_full, filled(t, f))
                    if panel == P_KVQ and b == 0:
                        V.tensor_copy(kT[:, CHUNK:], a[:]).then_inc(acc_free[f % 2], 1)
                    if panel == P_KVQ and b == 1:
                        dve.wait_ge(h_ready, t * 8 + 8)
                        V.tensor_copy(tmp2[:, 0, :], a[:]).then_inc(acc_free[f % 2], 1)
                    if panel == P_KZ:
                        V.tensor_copy(kb[:, b, :], a[:, 0:256])
                        V.tensor_copy(za[:, b, :], a[:, 256:256 + RANK]).then_inc(acc_free[f % 2], 1)
                    if panel == P_GA:
                        gate(f, b, ya[:, b, :])
                    if panel == P_GB:
                        gate(f, 4 + b, yb[:, b, :])
                    if s == 6:
                        dve.wait_ge(vT_full, t + 1)
                        V.tensor_copy(v[:, 1:, :].rearrange("p i c -> p (i c)"), ps_t[:, 0, :]).then_inc(v_ready, 1)
                        dve.wait_ge(stored, t * (16 * TB) + 16)
                        V.memset(probs[:, :, :, 0:CHUNK], 0.0)
                    if 0 <= s - 7 < 8:
                        bias_and_max(s - 7)
                    if 0 <= s - 9 < 8:
                        scale_and_gate(s - 9)
                    if 0 <= s - 8 < 8:
                        denominators(s - 8)
                    if s == 16:
                        dve.wait_ge(zaT_full, t + 1)
                        V.tensor_copy(zaT[0:RANK, :], ps_t[0:RANK, 0, :]).then_inc(zaT_ready, 1)
                    if s == 18:
                        dve.wait_ge(log_ready, t + 1)
                        V.scalar_tensor_tensor(la[:], ps_s[:], 0.0, lscr[:], ALU.min, ALU.subtract).then_inc(la_ready, 1)
                        V.tensor_copy(kT[:, 0:CHUNK], kT[:, NT:NT + CHUNK])
                        V.tensor_copy(v[:, 0, :], v[:, TB, :])
                        link(V.tensor_copy(dist[:, 0, :], dist[:, 1, :]), t)
                    if s == 19:
                        dve.wait_ge(decay_ready, t + 1)
                        V.tensor_tensor(kb[:], kb[:], lscr[:], ALU.mult).then_inc(kb_ready, 1)
                    if 20 <= s < 24:
                        update_state(s - 20)
                        y_low(s - 20)
                    if 21 <= s < 25:
                        i = s - 21
                        freed(first_fill(4 * P_GB + i))
                        dve.wait_ge(o_squared, t * 4 + (i + 1))
                        for low, o in enumerate((ps_o, ps_y)):
                            heads = yb[:, i, :].rearrange("p (h l e) -> p l h e", l=2, e=B_V)[:, low]
                            last = V.tensor_tensor(heads, heads, o[:, 0:256].rearrange("p (h e) -> p h e", e=B_V), ALU.mult)
                        last.then_inc(o_gated, 1)
                    if s == 25:
                        dve.wait_ge(o_squared, t * 4 + 4)
                        rsqrt(rs_o, ssq_o, B_V, 4 * TB, t)
                        dve.wait_ge(o_gated, t * 4 + 4)
                        yb3 = yb[:].rearrange("p i (h e) -> p (i h) e", e=B_V)
                        V.tensor_tensor(yb3, yb3, rs_o.unsqueeze(2).to_broadcast([P, 4 * TB, B_V]), ALU.mult
                                        ).then_inc(yb_ready, 1)
                    if 27 <= s < 31:
                        y_low(s - 23)
                    if panel in P_BR:
                        merge(s, P_BR.index(panel), b)
                    if s == 55:
                        normalise((2,))
                    if panel in P_OUT:
                        cols = slice(P_OUT.index(panel) * 512, P_OUT.index(panel) * 512 + 512)
                        if panel == P_OUT[0]:
                            dve.wait_ge(res_loaded[b], t * 16 + 16)
                        n = 4 * P_OUT.index(panel) + b
                        if n >= 2:
                            dve.wait_ge(res_ready, t * 8 + (n - 1))
                        dve.wait_ge(acc_full, filled(t, f))
                        V.tensor_tensor(tmp[:, b % 2, :], a[:], gate_row[:, cols], ALU.mult).then_inc(acc_free[f % 2], 1)
                        freed(f)
                        V.tensor_tensor(res[:, b, cols], res[:, b, cols], tmp[:, b % 2, :], ALU.add).then_inc(res_ready, 1)
                    if s == 50:
                        x_scale(t + 1, t)
                    if 51 <= s < 55:
                        k = 2 * (s - 51)
                        if k:
                            dve.wait_ge(h_ready, (t + 1) * KB_D + (k - 1))
                        affine(t + 1, k, ps_t[:, 0, :], h_plain[0])
                        h_low(t + 1, k, h_plain[0])
                        h_low(t + 1, k + 1, h_plain[1])
                    if s == 54:
                        normalise((0, 1))
                    if s == 55:
                        normalise((3,))
                assert steps[0] == DVE_TILE, steps

        @block.scalar
        def _(act):
            A = nc.scalar.activation
            steps = [0]
            ACT_BEFORE, ACT_TILE = 3, 5

            def link(ins, t=None):
                ins.then_inc(act_step, 1)
                steps[0] += 1
                if t is None:
                    act.wait_ge(act_step, steps[0])
                else:
                    act.wait_ge(act_step, t * ACT_TILE + (ACT_BEFORE + steps[0]))

            act.sem_inc(stored, 16)
            for dst, src in ((modb, ada_b), (norm_col, norm_g), (half_g, head_g),
                             (sink8, sinks.partition_broadcast(P)),
                             (ident[:], ident_in), (suffix[:], suffix_in), (chunks[:], chunks_in), (dist[:], dist_in),
                             (gate_row[:], ada_b_row.partition_broadcast(P)),
                             (final_row[:], final_g.partition_broadcast(P))):
                act.dma_start(dst, src).then_inc(consts_loaded, 16)
            act.dma_start(w_al[0:RANK, :], w_alpha).then_inc(consts_loaded, 16)
            act.dma_start(w_al[RANK:RANK + 1, :], b_alpha).then_inc(consts_loaded, 16)
            act.wait_ge(c_loaded, 16)
            A(c_tanh, c_col, ACT.Tanh, scale=0.5).then_inc(c_tanh_done, 1)

            def x_square(T, t, blocks=(0, 1, 2, 3)):
                junk = squares[:] if t is not None else tmp2[:].rearrange("p a n -> p (a n)")
                for i in blocks:
                    act.wait_ge(x_loaded[i], 16 * T + 16)
                    square = A(junk, xn[:, i, :], ACT.Square, accum_out=ssq_x[:, i:i + 1])
                    if i == 3:
                        square.then_inc(x_squared, 1)
                    else:
                        link(square, t)

            def affine(T, k, bank, buf):
                act.wait_ge(xT_full, T * KB_D + (k + 1))
                A(buf, bank, ACT.Identity, bias=shift[:, k:k + 1], scale=gscale[:, k:k + 1]).then_inc(xT_read[1], 1)

            def h_high(T, k, buf):
                act.wait_ge(xT_read[k % 2], T * 4 + (k // 2 + 1))
                A(h_hi[:, k, :], buf, ACT.Copy).then_inc(h_hi_ready, 1)

            x_square(0, None)
            act.wait_ge(ss_loaded[-1][KB_D - 3], 16)
            for k in range(KB_D):
                act.dma_start(ada_gt[k][:], ada_w[k * P:(k + 1) * P, 2 * D:3 * D]).then_inc(gt_loaded[k], 16)
            for k in range(0, KB_D, 2):
                act.wait_ge(gscale_ready, 1 + (k + 1) // 4)
                if k >= 4:
                    act.wait_ge(h_ready, k - 2)
                affine(0, k + 1, first_banks[k + 1], h_plain[(k + 1) % 4])
                h_high(0, k, h_plain[k % 4])
                h_high(0, k + 1, h_plain[(k + 1) % 4])

            assert steps[0] == ACT_BEFORE, steps
            steps[0] = 0

            with act.Fori(0, TILES) as t:
                for s in range(SLOTS):
                    panel, b = s // 4, s % 4
                    f = first_fill(s)
                    a = acc[f % 2]
                    if panel in (P_QA, P_VB, P_GA, P_GB) + P_ZM or panel == P_KVQ and b >= 2:
                        act.wait_ge(acc_full, filled(t, f))
                    if panel == P_QA:
                        A(qT[:, b, :], a[:], ACT.Copy).then_inc(acc_free[f % 2], 1)
                    if panel == P_KVQ and b >= 2:
                        A(qbT[:, b - 2, :], a[:], ACT.Copy, scale=B_K ** -0.5).then_inc(acc_free[f % 2], 1)
                    if panel == P_VB:
                        A(vb[:, b, :], a[:], ACT.Copy).then_inc(acc_free[f % 2], 1)
                    if panel in (P_GA, P_GB):
                        A(tmp[:, b % 2, :], a[:], ACT.Tanh, scale=0.5).then_inc(gate_tanh, 1)
                    if panel in P_ZM:
                        dst = (gate_a, gate_b)[P_ZM.index(panel) % 2]
                        A(dst[:, b, :], a[:], ACT.Tanh, scale=0.5).then_inc(acc_free[f % 2], 1)
                    if 0 <= s - 8 < 8:
                        u = s - 8
                        act.wait_ge(ptrans_full, t * 8 + (u + 1))
                        A(probsT[:, u % 2, 0, :, :].rearrange("p j q -> p (j q)"), ps_t[:, 0, :], ACT.Copy
                          ).then_inc(ptrans_act, 1)
                    if 0 <= s - 7 < 8:
                        u = s - 7
                        act.wait_ge(negmax, t * 8 + (u + 1))
                        for j in range(A_GROUP):
                            pr = probs[:, u % 2, j, CHUNK:256]
                            A(pr, pr, ACT.Exp, bias=nmax[:, u, j:j + 1], scale=1.0 / SINK_SCALE,
                              accum_out=sums[:, u, j:j + 1])
                        A(esink[:, u, :], esink[:, u, :], ACT.Exp, scale=1.0 / SINK_SCALE).then_inc(probs_ready, 1)
                    if s == 17:
                        act.wait_ge(z_full, t + 1)
                        link(A(lscr[:], ps_s[:], ACT.Abs), t)
                        link(A(lscr[:], lscr[:], ACT.Exp, scale=-1.0), t)
                        A(lscr[:], lscr[:], ACT.Ln, bias=1.0).then_inc(log_ready, 1)
                    if s == 19:
                        act.wait_ge(cum_full, t + 1)
                        A(lscr[:], ps_s[:], ACT.Exp)
                        A(decay, ps_y[:, 0:16], ACT.Exp).then_inc(decay_ready, 1)
                    if 21 <= s < 25:
                        i = s - 21
                        if i:
                            act.wait_ge(o_squared, t * 4 + i)
                        act.wait_ge(o_full, t * 4 + (i + 1))
                        for hd in range(B_HEADS):
                            hp, low = hd // 2, hd % 2
                            last = A(tmp2[:, 0, hd * B_V:(hd + 1) * B_V],
                                     (ps_o, ps_y)[low][:, hp * B_V:(hp + 1) * B_V], ACT.Square,
                                     accum_out=ssq_o[:, i * 4 + hd:i * 4 + hd + 1])
                        last.then_inc(o_squared, 1)
                    if 20 <= s < 24 or 27 <= s < 31:
                        n = s - 20 if s < 24 else s - 23
                        act.wait_ge(yT_full, t * 8 + (n + 1))
                        A(y_hi[:, n, :], ps_t[:, n % 2, :], ACT.Identity, scale=0.5 if n < 4 else half_g
                          ).then_inc(yT_hi_ready, 1)
                    if panel in P_BR:
                        n = 4 * P_BR.index(panel) + b
                        act.wait_ge(m_plain, t * 8 + (n + 1))
                        A(m_hi[:, n, :], tmp[:, b % 2, :], ACT.Copy).then_inc(m_hi_ready, 1)
                    if s == 4 * P_BR[1] + 2:
                        act.wait_ge(m_ready, t * 8 + 6)
                        for i in (0, 2):
                            act.dma_start(xn[:, i, :], x_block((t + 1) % TILES, i)).then_inc(x_loaded[i], 16)
                    if s == 4 * P_BR[1] + 3:
                        act.wait_ge(m_ready, t * 8 + 8)
                        act.dma_start(res[:, 0, :], x_block(t, 0)).then_inc(res_loaded[0], 16)
                        for i in (1, 3):
                            act.dma_start(xn[:, i, :], x_block((t + 1) % TILES, i)).then_inc(x_loaded[i], 16)
                        for i in (1, 2, 3):
                            act.dma_start(res[:, i, :], x_block(t, i)).then_inc(res_loaded[i], 16)
                    if s == 48:
                        x_square(t + 1, t, (0, 2))
                    if s == 49:
                        x_square(t + 1, t, (1, 3))
                    if 51 <= s < 55:
                        k = 2 * (s - 51)
                        if k:
                            act.wait_ge(h_ready, (t + 1) * KB_D + k)
                        affine(t + 1, k + 1, ps_t[:, 1, :], h_plain[1])
                        h_high(t + 1, k, h_plain[0])
                        h_high(t + 1, k + 1, h_plain[1])
                    if s >= 52:
                        i = s - 52
                        if i == 0:
                            act.wait_ge(x_squared, t + 2)
                        else:
                            act.wait_ge(res_squared, t * 4 + i)
                        act.wait_ge(res_ready, t * 8 + (5 + i))
                        A(squares[:], res[:, i, :], ACT.Square, accum_out=ssq_f[:, i:i + 1]).then_inc(res_squared, 1)
                assert steps[0] == ACT_TILE, steps
                for i in range(TB):
                    act.wait_ge(result_ready, t * 4 + (i + 1))
                    act.dma_start(out[bass.ds(t * NT + i * P, P), :], res[:, i, :]).then_inc(stored, 16)


def shape_constants():
    r = np.arange(P)
    ident = np.eye(P, dtype=np.float32)
    same = r[:, None] // CHUNK == r[None, :] // CHUNK
    suffix = (same & (r[:, None] > r[None, :])).astype(np.float32) / np.float32(16.0)
    chunks = (r[:, None] // CHUNK == np.arange(2)[None, :]).astype(np.float32) / np.float32(16.0)
    key = np.arange(WIN)
    d = np.abs(r[:, None] + CHUNK - key[None, :]).astype(np.float32)
    seen = (key[None, :] // CHUNK == r[:, None] // CHUNK) | (key[None, :] // CHUNK == r[:, None] // CHUNK + 1)
    inner = np.where(seen, d, np.float32(MASKED))
    first = np.where(seen & (key[None, :] >= CHUNK), d, np.float32(MASKED))
    dist = np.ascontiguousarray(np.stack([first, inner], axis=1).astype(np.float32))
    return ident, suffix, chunks, dist


def kernel(x, c, ada_w, ada_b, norm_g, w_in, w_alpha, b_alpha, sinks, head_norm_g,
           w_branch_a, w_branch_b, w_out, final_norm_g):
    from concourse import bacc
    from concourse.bass_utils import run_bass_kernel_spmd

    def columns(a):
        return np.ascontiguousarray(np.asarray(a).reshape(-1, P).T)

    a = {k: np.asarray(v) for k, v in dict(
        x=x, c=c, ada_w=ada_w, ada_b=ada_b, norm_g=norm_g, w_in=w_in, w_alpha=w_alpha, b_alpha=b_alpha, sinks=sinks,
        head_norm_g=head_norm_g, w_branch_a=w_branch_a, w_branch_b=w_branch_b, w_out=w_out,
        final_norm_g=final_norm_g).items()}
    ident, suffix, chunks, dist = shape_constants()
    inputs = [
        ("x", a["x"][0]), ("c", columns(a["c"][0])), ("ada_w", a["ada_w"][0]), ("ada_b", columns(a["ada_b"][0, :2 * D])),
        ("norm_g", columns(a["norm_g"][0])), ("w_in", a["w_in"][0]), ("w_alpha", a["w_alpha"][0]),
        ("b_alpha", a["b_alpha"]), ("sinks", a["sinks"][0]), ("head_g", columns(a["head_norm_g"][0])),
        ("w_br_a", a["w_branch_a"][0]), ("w_br_b", a["w_branch_b"][0]), ("w_out", a["w_out"][0]),
        ("final_g", a["final_norm_g"]), ("ada_b_row", a["ada_b"][0, 2 * D:]),
        ("ident", ident), ("suffix", suffix), ("chunks", chunks), ("dist", dist),
    ]
    nc = bacc.Bacc("TRN2", target_bir_lowering=False, num_devices=1)
    arrays, args = {}, []
    for name, value in inputs:
        value = np.ascontiguousarray(value)
        arrays["in_" + name] = value
        args.append(nc.dram_tensor("in_" + name, value.shape, mybir.dt.from_np(value.dtype), kind="ExternalInput").ap())
    out = nc.dram_tensor("out_0", (SEQ, D), mybir.dt.float32, kind="ExternalOutput").ap()
    build(nc, *args, out)
    r = run_bass_kernel_spmd(nc, [arrays], core_ids=[0])
    return np.asarray(r.results[0]["out_0"]).reshape(1, SEQ, D)
```

```python
import numpy as np
import concourse.bass as bass
from concourse import mybir

P = 128
D = 1024
SEQ = 2048
NT = 512
TILES = SEQ // NT
KB_D = D // P
TB = NT // P
CHUNK = 64
A_HEADS, A_GROUP, A_DIM = 8, 4, 64
WIN = 2 * CHUNK
B_HEADS, B_K, B_V = 4, 64, 128
RANK = 16
EPS = 1e-6
MASKED = 1e33
SINK_SCALE = 8.0
RSQRT_MAGIC = 0x5F3759DF

QA, KA, VA, GA, QB, KB, VB, GB, ZA, ZM = 0, 512, 640, 768, 1280, 1536, 1792, 2304, 2816, 2832
PANELS = [
    ("w_in", [(QA, 512)]),
    ("w_in", [(KA, 256), (QB, 256)]),
    ("w_in", [(GA, 512)]),
    ("w_in", [(KB, 256), (ZA, RANK)]),
    ("w_in", [(VB, 512)]),
    ("w_in", [(GB, 512)]),
    ("w_in", [(ZM, 512)]),
    ("w_in", [(ZM + D, 512)]),
    ("w_br", [(0, 512)]),
    ("w_in", [(ZM + 512, 512)]),
    ("w_in", [(ZM + D + 512, 512)]),
    ("w_br", [(512, 512)]),
    ("w_out", [(0, 512)]),
    ("w_out", [(512, 512)]),
]
P_QA, P_KVQ, P_GA, P_KZ, P_VB, P_GB = range(6)
P_ZM = (6, 7, 9, 10)
P_BR = (8, 11)
P_OUT = (12, 13)
SLOTS = 4 * len(PANELS)
DUOS = 4 * len(PANELS)
RING = 7
STAGES = 2
WIDTH = [sum(n for _, n in cols) for _, cols in PANELS]
FILLS = SLOTS + 8
MOD_GROUPS = [(0, D), (D, D + 512), (D + 512, 2 * D)]
DVE_BLOCKS = 4


def first_fill(slot):
    return slot + sum(min(max(slot - 4 * p, 0), 4) for p in P_BR)


def build(nc, x, c, ada_w, ada_b, norm_g, w_in, w_alpha, b_alpha, sinks, head_g, w_br_a, w_br_b, w_out,
          final_g, ada_b_row, ident_in, suffix_in, chunks_in, dist_in, out):
    F32, F32R, I32 = mybir.dt.float32, mybir.dt.float32r, mybir.dt.int32
    ACT, ALU, AX = mybir.ActivationFunctionType, mybir.AluOpType, mybir.AxisListType
    KIB = 1024

    cursor = [(nc.sbuf_base + 63) // 64 * 64]

    def place(name, shape, dt=F32, at=None):
        size = 4 * int(np.prod(shape[1:]))
        offset = cursor[0] if at is None else at
        if at is None:
            cursor[0] += (size + 31) // 32 * 32
        return nc.alloc_sbuf_tensor_at(name, shape, dt, offset=offset)

    def region(kib):
        at = cursor[0]
        cursor[0] += kib * KIB
        return at

    r_h, r_y, r_qv, r_hi, r_lo = region(32), region(32), region(16), region(16), region(16)
    h_hi = place("h_hi", [P, KB_D, NT], F32R, at=r_h)
    h_lo = place("h_lo", [P, KB_D, NT], F32R, at=r_h + 16 * KIB)
    y_hi = place("y_hi", [P, 8, NT], F32R, at=r_y)
    y_lo = place("y_lo", [P, 8, NT], F32R, at=r_y + 16 * KIB)
    probs = place("probs", [P, 2, A_GROUP, WIN], at=r_y + 8 * KIB)
    v_win = place("v_win", [P, 2, TB, P], at=r_y + 12 * KIB)
    probsT = place("probsT", [P, 2, A_GROUP, P], at=r_y + 24 * KIB)
    res = place("res", [P, TB, D], at=r_y)
    squares = place("squares", [P, D], at=r_y + 16 * KIB)
    qT = place("qT", [P, 4, NT], at=r_qv)
    vb = place("vb", [P, TB, 512], at=r_qv + 8 * KIB)
    gate_a = place("gate_a", [P, 4, NT], at=r_qv)
    gate_b = place("gate_b", [P, 4, NT], at=r_qv + 8 * KIB)
    xn = place("xn", [P, TB, D], at=r_qv)
    ya = place("ya", [P, TB, 512], at=r_hi)
    yb = place("yb", [P, TB, 512], at=r_hi + 8 * KIB)
    m_hi = place("m_hi", [P, KB_D, NT], F32R, at=r_hi)
    qbT = place("qbT", [P, 2, NT], at=r_lo)
    kb = place("kb", [P, TB, 256], at=r_lo + 4 * KIB)
    la = place("la", [P, TB, 256], at=r_lo + 8 * KIB)
    lscr = place("lscr", [P, TB, 256], at=r_lo + 12 * KIB)
    m_lo = place("m_lo", [P, KB_D, NT], F32R, at=r_lo)
    w_hi_at, w_lo_at = region(4 * RING), region(4 * RING)
    w_split_hi = place("w_split_hi", [P, RING, 2, 512], F32R, at=w_hi_at)
    w_split_lo = place("w_split_lo", [P, RING, 2, 512], F32R, at=w_lo_at)
    ss_at = [r_y, r_y + 16 * KIB, w_hi_at + 4 * KIB * (RING - 4), w_lo_at + 4 * KIB * (RING - 4)]
    ada_ss = [place(f"ada_ss{k}", [P, 2 * D], at=ss_at[k // 2] + 8 * KIB * (k % 2)) for k in range(KB_D)]
    ada_gt = [place(f"ada_gt{k}", [P, D], at=r_hi + 4 * KIB * k) for k in range(KB_D)]

    stage = [place(f"stage{i}", [P, 2, 512]) for i in range(STAGES)]
    kT = place("kT", [P, CHUNK + NT])
    vT = place("vT", [P, CHUNK + NT])
    state = place("state", [P, 4, 256])
    dist = place("dist", [P, 2, WIN])
    ident = place("ident", [P, P])
    suffix_r = place("suffix_r", [P, P], F32R)
    chunks = place("chunks", [P, 2])
    gate_row = place("gate_row", [P, D])
    final_row = place("final_row", [P, D])
    w_al = place("w_al", [RANK + 1, 256])
    zaT = place("zaT", [RANK + 1, NT])
    za = place("za", [P, TB, RANK])
    ones = state[:, 0, 0:P]
    tmp = place("tmp", [P, 2, 512])
    tmp2 = place("tmp2", [P, 2, 512])
    la_hi = place("la_hi", [P, TB, 256], F32R, at=cursor[0] - 8 * KIB)
    la_lo = place("la_lo", [P, TB, 256], F32R, at=cursor[0] - 4 * KIB)
    suffix = state[:, 1, 0:P]
    small = place("small", [P, 336])
    h_plain = [tmp2[:, 0, :], tmp2[:, 1, :], tmp[:, 0, :], tmp[:, 1, :]]
    assert cursor[0] <= nc.sbuf_usable_end, cursor[0]

    used = [0]

    def cell(n):
        a = used[0]
        used[0] += n
        return small[:, a:a + n]

    c_col, c_tanh, c_silu = cell(8), cell(8), cell(8)
    shift, gscale, modb, norm_col = cell(8), cell(8), cell(16), cell(8)
    half_g, sink8 = cell(1), cell(8)
    maxs, nmax, esink, sums, rden = (cell(32).rearrange("p (u j) -> p u j", j=4) for _ in range(5))
    decay = cell(16)
    ssq_x, ssq_o, ssq_f = cell(4), cell(16), cell(4)
    rs_x, rs_o, rs_f = cell(4), cell(16), cell(4)
    rs_m, rs_t = cell(16), cell(16)
    assert used[0] <= 336, used

    def psum(name, shape):
        return nc.alloc_psum_tensor(name, shape, F32)

    acc = [psum(f"acc{i}", [P, 512]) for i in range(2)]
    ps_s = psum("ps_s", [P, 4, 256])
    ps_t = psum("ps_t", [P, 2, 512])
    ps_y = psum("ps_y", [P, 512])
    ps_o = psum("ps_o", [P, 512])

    first_banks = [ps_t[:, 0, :], ps_t[:, 1, :], ps_s[:, 0:2, :].rearrange("p a n -> p (a n)"),
                   ps_s[:, 2:4, :].rearrange("p a n -> p (a n)"), ps_y[:], ps_o[:], ps_t[:, 0, :], ps_t[:, 1, :]]

    mod_banks = [(ps_y[:], ps_o[:]), (acc[0][:],), (acc[1][:],)]

    names = """consts_loaded rows_loaded ident_loaded c_loaded stored
        w_ready w_used acc_full
        c_tanh_done silu_ready ss_summed shift_full scale_full shift_ready gt_summed gscale_ready gate_full gate_ready
        x_squared x_scaled xT_full h_hi_ready h_ready
        gate_tanh vT_full v_ready
        scores_full scores_read negmax probs_ready ptrans_full ptrans_read pv_full y_scaled
        zaT_full zaT_ready z_full log_ready la_ready la_hi_ready la_split cum_full decay_ready kb_ready kv_full state_ready
        o_full o_squared o_gated yb_ready yT_full yT_hi_ready yT_ready
        m_plain m_hi_ready m_ready res_ready res_squared result_ready
        dve_step act_step pool_step pe_turn pool_turn""".split()
    S = {n: nc.alloc_semaphore(n) for n in names}
    acc_free = [nc.alloc_semaphore(f"acc_free{i}") for i in range(2)]
    xT_read = [nc.alloc_semaphore(f"xT_read{i}") for i in range(2)]
    x_loaded = [nc.alloc_semaphore(f"x_loaded{i}") for i in range(TB)]
    res_loaded = [nc.alloc_semaphore(f"res_loaded{i}") for i in range(TB)]
    ss_loaded = [[nc.alloc_semaphore(f"ss_loaded{n}_{k}") for k in range(KB_D)] for n in range(len(MOD_GROUPS))]
    gt_loaded = [nc.alloc_semaphore(f"gt_loaded{k}") for k in range(KB_D)]
    stage_loaded = [nc.alloc_semaphore(f"stage_loaded{i}") for i in range(STAGES)]
    (consts_loaded, rows_loaded, ident_loaded, c_loaded, stored,
     w_ready, w_used, acc_full,
     c_tanh_done, silu_ready, ss_summed, shift_full, scale_full, shift_ready, gt_summed, gscale_ready, gate_full, gate_ready,
     x_squared, x_scaled, xT_full, h_hi_ready, h_ready,
     gate_tanh, vT_full, v_ready,
     scores_full, scores_read, negmax, probs_ready, ptrans_full, ptrans_read, pv_full, y_scaled,
     zaT_full, zaT_ready, z_full, log_ready, la_ready, la_hi_ready, la_split, cum_full, decay_ready, kb_ready, kv_full, state_ready,
     o_full, o_squared, o_gated, yb_ready, yT_full, yT_hi_ready, yT_ready,
     m_plain, m_hi_ready, m_ready, res_ready, res_squared, result_ready,
     dve_step, act_step, pool_step, pe_turn, pool_turn) = (S[n] for n in names)

    CONSTS = 9
    def may_fill(t, f):
        return t * (FILLS // 2) + (f // 2 + 1)

    def filled(t, f):
        return t * FILLS + (f + 1)

    def w_src(panel, duo):
        matrix = PANELS[panel][0]
        if matrix == "w_br":
            return (w_br_a if duo < 2 else w_br_b), 2 * P * (duo % 2)
        return (w_in if matrix == "w_in" else w_out), 2 * P * duo

    loads_of = [len(PANELS[d // 4][1]) for d in range(DUOS)]
    loads_upto = [sum(n for e, n in enumerate(loads_of[:d + 1]) if e % STAGES == d % STAGES) for d in range(DUOS)]
    loads_tile = [sum(n for e, n in enumerate(loads_of) if e % STAGES == i) for i in range(STAGES)]

    def x_block(t, i):
        return x[bass.ds(t * NT + i * P, P), :]

    block = nc.Block()
    with block:
        @block.sync
        def _(sp):
            sp.dma_start(c_col, c).then_inc(c_loaded, 16)
            sp.dma_start(ident[:], ident_in).then_inc(ident_loaded, 16)
            for i in range(TB):
                sp.dma_start(xn[:, i, :], x[i * P:(i + 1) * P, :]).then_inc(x_loaded[i], 16)

            def load_duo(d):
                src, row = w_src(d // 4, d % 4)
                col = 0
                for first, n in PANELS[d // 4][1]:
                    sp.dma_start(stage[d % STAGES][:, :, col:col + n],
                                 src[row:row + 2 * P, first:first + n].rearrange("(k p) n -> p k n", p=P)
                                 ).then_inc(stage_loaded[d % STAGES], 16)
                    col += n

            for n, (m0, m1) in enumerate(MOD_GROUPS):
                if n == 1:
                    for d in range(STAGES):
                        load_duo(d)
                for k in range(KB_D):
                    sp.dma_start(ada_ss[k][:, m0:m1], ada_w[k * P:(k + 1) * P, m0:m1]).then_inc(ss_loaded[n][k], 16)
            with sp.Fori(0, TILES) as t:
                for d in range(STAGES, DUOS + STAGES):
                    sp.wait_ge(w_ready, t * DUOS + (d - STAGES + 1))
                    load_duo(d % DUOS)
            for xl in x_loaded:
                sp.wait_ge(xl, 16 * (TILES + 1))
            for i in range(STAGES):
                sp.wait_ge(stage_loaded[i], TILES * (16 * loads_tile[i]) + 16 * loads_upto[i])
            sp.wait_ge(stored, 16 + 16 * TB * TILES)

        @block.gpsimd
        def _(pool):
            with pool.Fori(0, TILES) as t:
                for d in range(DUOS):
                    n, r, s = WIDTH[d // 4], d % RING, d % STAGES
                    pool.wait_ge(stage_loaded[s], t * (16 * loads_tile[s]) + 16 * loads_upto[d])
                    pool.wait_ge(w_used, t * DUOS + (d + 1))
                    pool.sem_inc(pool_turn, 1)
                    if d // 4 == P_QA:
                        def split_as(z, k):
                            return z[:, r, k, :].rearrange("p (j g e) -> p j g e", g=2, j=4)
                        parts = [(split_as(w_split_hi, k), split_as(w_split_lo, k),
                                  stage[s][:, k, :].rearrange("p (g j e) -> p j g e", g=2, j=4)) for k in range(2)]
                    else:
                        parts = [(w_split_hi[:, r, :, :n], w_split_lo[:, r, :, :n], stage[s][:, :, :n])]
                    for hi, _, raw in parts:
                        last = nc.gpsimd.tensor_scalar(hi, raw, 1.0, 1.0, ALU.mult, ALU.mult)
                    last.then_inc(pool_step, 1)
                    pool.wait_ge(pool_step, t * DUOS + (d + 1))
                    for hi, lo, raw in parts:
                        last = nc.gpsimd.tensor_tensor(lo, raw, hi.bitcast(F32), ALU.subtract)
                    last.then_inc(w_ready, 1)

        @block.tensor
        def _(pe):
            mm = nc.tensor.matmul

            def x_transpose(bank, T, k):
                for i in range(TB):
                    last = nc.tensor.transpose(bank[:, i * P:(i + 1) * P], xn[:, i, k * P:(k + 1) * P], ident[:])
                last.then_inc(xT_full, 1)

            pe.sem_inc(w_used, RING - 4)
            pe.wait_ge(silu_ready, 1)

            def weigh(n):
                m0, m1 = MOD_GROUPS[n]
                for k in range(DVE_BLOCKS, KB_D):
                    pe.wait_ge(ss_loaded[n][k], 16)
                    for bank, a in zip(mod_banks[n], range(m0, m1, 512)):
                        mm(bank, c_silu[:, k:k + 1].to_broadcast([P, P]), ada_ss[k][:, a:a + 512],
                           start=k == DVE_BLOCKS, stop=False)
                pe.wait_ge(ss_summed, n + 1)
                for bank, a in zip(mod_banks[n], range(m0, m1, 512)):
                    last = mm(bank, ones, ada_ss[0][:, a:a + 512], start=False, stop=True)
                return last

            weigh(0).then_inc(shift_full, 1)
            pe.wait_ge(ident_loaded, 16)
            pe.wait_ge(x_scaled, 1)
            for k in range(4):
                x_transpose(first_banks[k], 0, k)
            weigh(1).then_inc(scale_full, 1)
            pe.wait_ge(shift_ready, 1)
            for k in (4, 5):
                x_transpose(first_banks[k], 0, k)
            weigh(2).then_inc(scale_full, 1)
            pe.wait_ge(scale_full, 2)
            pe.sem_inc(w_used, 3)
            pe.wait_ge(consts_loaded, 16 * CONSTS)
            for k in (6, 7):
                pe.wait_ge(xT_read[k % 2], 1)
                x_transpose(first_banks[k], 0, k)

            with pe.Fori(0, TILES) as t:
                def three(o, a_hi, a_lo, b_hi, b_lo, start, stop):
                    first = mm(o, a_hi, b_hi, start=start, stop=False)
                    mm(o, a_hi, b_lo, start=False, stop=False)
                    return first, mm(o, a_lo, b_hi, start=False, stop=stop)

                def weights(panel, k, cols):
                    r = (4 * panel + k // 2) % RING
                    return w_split_hi[:, r, k % 2, cols], w_split_lo[:, r, k % 2, cols]

                def fill(f, panel, ks, first, last_fill, step, ready=None):
                    pe.wait_ge(acc_free[f % 2], may_fill(t, f))
                    for k in ks:
                        duo = 4 * panel + k // 2
                        if first and k % 2 == 0:
                            pe.wait_ge(w_ready, t * DUOS + (duo + 1))
                        if ready is not None and k == ks[0] or ready is not None and ready[2]:
                            pe.wait_ge(ready[0], t * 8 + ready[1](k))
                        product, last = step(k, k == ks[0], k == ks[-1])
                        if first and k == 0:
                            product.then_inc(w_used, 1)
                        if last_fill and k % 2 and k != ks[-1]:
                            last.then_inc(w_used, 1)
                        if last_fill and k == 4 and ks[0] == 4:
                            product.then_inc(w_used, 1)
                    last.then_inc(acc_full, 1)

                def transposed(panel, f, c0, b, ks, first, last_fill, ready=None):
                    b_hi, b_lo = b

                    def step(k, start, stop):
                        w_hi, w_lo = weights(panel, k, slice(c0, c0 + P))
                        return three(acc[f % 2][:], w_hi, w_lo, b_hi[:, k, :], b_lo[:, k, :], start, stop)

                    fill(f, panel, ks, first, last_fill, step, ready)

                def by_token(panel, f, i, n, a, first, last_fill, ready=None):
                    a_hi, a_lo = a
                    tok = slice(i * P, (i + 1) * P)

                    def step(k, start, stop):
                        w_hi, w_lo = weights(panel, k, slice(0, n))
                        return three(acc[f % 2][:, :n], a_hi[:, k, tok], a_lo[:, k, tok], w_hi, w_lo, start, stop)

                    fill(f, panel, ks_all, first, last_fill, step, ready)

                def evacuated(f):
                    pe.wait_ge(acc_free[f % 2], may_fill(t, f) + 1)

                ks_all = list(range(KB_D))
                h = (h_hi, h_lo)

                def dense(s):
                    panel, b = s // 4, s % 4
                    f = first_fill(s)
                    first, last_fill = b == 0, b == 3
                    if panel == P_QA:
                        transposed(panel, f, b * P, h, ks_all, first, last_fill,
                                   ready=(h_ready, lambda k: k + 1, True) if first else None)
                    elif panel == P_KVQ:
                        transposed(panel, f, b * P, h, ks_all, first, last_fill)
                    elif panel in (P_GA, P_KZ, P_VB, P_GB):
                        by_token(panel, f, b, WIDTH[panel], h, first, last_fill)
                    elif panel in P_ZM:
                        transposed(panel, f, b * P, h, ks_all, first, last_fill)
                    elif panel in P_BR:
                        y = (y_hi, y_lo)
                        pair = P_BR.index(panel) == 0 and first
                        transposed(panel, f, b * P, y, ks_all[:4], first, last_fill,
                                   ready=(yT_ready, lambda k: 4, False) if pair else None)
                        transposed(panel, f + 1, b * P, y, ks_all[4:], first, last_fill,
                                   ready=(yT_ready, lambda k: 8, False) if pair else None)
                    else:
                        by_token(panel, f, b, 512, (m_hi, m_lo), first, last_fill,
                                 ready=(m_ready, lambda k: k + 1, True) if panel == P_OUT[0] and first else None)

                def scores(u):
                    pair, g = u // 2, u % 2
                    if u == 0:
                        pe.wait_ge(gate_ready, 1)
                        evacuated(3)
                        evacuated(first_fill(4 * P_KVQ))
                    else:
                        pe.wait_ge(scores_read, t * 8 + u)
                    pe.sem_inc(pe_turn, 1)
                    rows = slice(g * A_DIM, (g + 1) * A_DIM)
                    for j in range(A_GROUP):
                        for c2 in range(2):
                            at = pair * P + c2 * CHUNK
                            last = mm(ps_s[c2 * CHUNK:(c2 + 1) * CHUNK, j, 0:WIN], qT[rows, j, at:at + CHUNK],
                                      kT[rows, at:at + WIN], start=True, stop=True)
                    last.then_inc(scores_full, 1)

                def adaln_gate():
                    pe.wait_ge(gt_summed, 1)
                    for half in range(2):
                        last = mm(ps_s[:, 2 * half:2 * half + 2, :], ones, ada_gt[0][:, half * 512:half * 512 + 512],
                                  start=True, stop=True)
                    last.then_inc(gate_full, 1)

                def v_transpose():
                    evacuated(first_fill(4 * P_KVQ + 1))
                    for c2 in range(2):
                        for i in range(TB):
                            at = i * P + c2 * CHUNK
                            last = nc.tensor.transpose(ps_t[:, c2, i * P:(i + 1) * P], vT[:, at:at + WIN], ident[:])
                    last.then_inc(vT_full, 1)

                def transpose_probs(u):
                    pe.wait_ge(probs_ready, t * 8 + (u + 1))
                    if u == 0:
                        pe.wait_ge(v_ready, t + 1)
                    if u >= 2:
                        pe.wait_ge(ptrans_read, t * 8 + (u - 1))
                    for j in range(A_GROUP):
                        last = nc.tensor.transpose(ps_t[:, u % 2, j * P:(j + 1) * P], probs[:, u % 2, j, :], ident[:])
                    last.then_inc(ptrans_full, 1)

                def attend(u):
                    pair, g = u // 2, u % 2
                    if u == 0:
                        pe.wait_ge(v_ready, t + 1)
                    else:
                        pe.wait_ge(y_scaled, t * 8 + u)
                    pe.wait_ge(ptrans_read, t * 8 + (u + 1))
                    vc = slice(g * A_DIM, (g + 1) * A_DIM)
                    for j in range(A_GROUP):
                        for c2 in range(2):
                            queries = slice(c2 * CHUNK, (c2 + 1) * CHUNK)
                            last = mm(ps_y[queries, j * A_DIM:(j + 1) * A_DIM], probsT[:, u % 2, j, queries],
                                      v_win[:, c2, pair, vc], start=True, stop=True)
                    last.then_inc(pv_full, 1)

                def y_transpose(n):
                    if n == 0:
                        pe.wait_ge(y_scaled, t * 8 + 8)
                    if n == 4:
                        pe.wait_ge(yb_ready, t + 1)
                    if n >= 2:
                        pe.wait_ge(yT_ready, t * 8 + (n - 1))
                    src = ya if n < 4 else yb
                    for i in range(TB):
                        last = nc.tensor.transpose(ps_t[:, n % 2, i * P:(i + 1) * P],
                                                   src[:, i, (n % 4) * P:(n % 4 + 1) * P], ident[:])
                    last.then_inc(yT_full, 1)

                def za_transpose():
                    evacuated(first_fill(4 * P_KZ + 2))
                    evacuated(first_fill(4 * P_KZ + 3))
                    for i in range(TB):
                        last = nc.tensor.transpose(ps_t[0:RANK, 0, i * P:(i + 1) * P], za[:, i, :], ident[:])
                    last.then_inc(zaT_full, 1)

                def decay_logits():
                    pe.wait_ge(zaT_ready, t + 1)
                    pe.wait_ge(scores_read, t * 8 + 8)
                    for i in range(TB):
                        last = mm(ps_s[:, i, :], zaT[:, i * P:(i + 1) * P], w_al[:], start=True, stop=True)
                    last.then_inc(z_full, 1)

                def suffix_sums():
                    pe.wait_ge(la_split, t + 1)
                    pe.wait_ge(y_scaled, t * 8 + 8)
                    for i in range(0, TB, 2):
                        for part in (la_hi, la_lo):
                            mm(ps_s[:, i:i + 2, :], suffix_r[:], part[:, i:i + 2, :], start=part is la_hi, stop=part is la_lo)
                    for i in range(TB):
                        for hp in range(2):
                            a = hp * 8 + 2 * i
                            last = mm(ps_y[:, a:a + 2], la[:, i, hp * P:(hp + 1) * P], chunks[:], start=True, stop=True)
                    last.then_inc(cum_full, 1)

                def key_values(i):
                    if i == 0:
                        pe.wait_ge(kb_ready, t + 1)
                        evacuated(first_fill(4 * P_VB + 2))
                        evacuated(first_fill(4 * P_VB + 3))
                    else:
                        pe.wait_ge(state_ready, t * 4 + i)
                    pe.sem_inc(pe_turn, 1)
                    for c2 in range(2):
                        rows = slice(c2 * CHUNK, (c2 + 1) * CHUNK)
                        for hd in range(B_HEADS):
                            hp, low = hd // 2, hd % 2
                            last = mm(ps_s[low * B_K:(low + 1) * B_K, 2 * c2, hp * P:(hp + 1) * P], kb[rows, i, hd * B_K:(hd + 1) * B_K],
                                      vb[rows, i, hd * B_V:(hd + 1) * B_V], start=True, stop=True)
                    last.then_inc(kv_full, 1)

                def read_state(i):
                    pe.wait_ge(state_ready, t * 4 + (i + 1))
                    if i == 0:
                        evacuated(first_fill(4 * P_KVQ + 2))
                        evacuated(first_fill(4 * P_KVQ + 3))
                    else:
                        pe.wait_ge(o_gated, t * 4 + i)
                    pe.sem_inc(pe_turn, 1)
                    for c2 in range(2):
                        tok = slice(i * P + c2 * CHUNK, i * P + (c2 + 1) * CHUNK)
                        for hd in range(B_HEADS):
                            hp, low = hd // 2, hd % 2
                            rows = slice(low * B_K, (low + 1) * B_K)
                            last = mm((ps_o, ps_y)[low][c2 * CHUNK:(c2 + 1) * CHUNK, hp * B_V:(hp + 1) * B_V],
                                      qbT[rows, hp, tok], state[rows, (2 * i + c2) % 4, hp * P:(hp + 1) * P],
                                      start=True, stop=True)
                    last.then_inc(o_full, 1)

                for s in range(SLOTS):
                    dense(s)
                    if 0 <= s - 7 < 8:
                        scores(s - 7)
                    if 0 <= s - 9 < 8:
                        attend(s - 9)
                    if 0 <= s - 8 < 8:
                        transpose_probs(s - 8)
                    if s == 4:
                        with pe.If(t == 0):
                            adaln_gate()
                    if s == 6:
                        v_transpose()
                    if s == 16:
                        za_transpose()
                    if s == 17:
                        decay_logits()
                    if s == 19:
                        suffix_sums()
                    if 20 <= s < 24:
                        y_transpose(s - 20)
                        key_values(s - 20)
                    if 21 <= s < 25:
                        read_state(s - 21)
                    if 27 <= s < 31:
                        y_transpose(s - 23)
                    if 51 <= s < 55:
                        for k in (2 * (s - 51), 2 * (s - 51) + 1):
                            if k == 0:
                                pe.wait_ge(x_scaled, (t + 1) + 1)
                            if k >= 2:
                                pe.wait_ge(xT_read[k % 2], (t + 1) * 4 + k // 2)
                            x_transpose(ps_t[:, k % 2, :], t + 1, k)

        @block.vector
        def _(dve):
            V = nc.vector
            steps = [0]
            DVE_BEFORE, DVE_TILE = 42, 91

            def link(ins, t=None):
                ins.then_inc(dve_step, 1)
                steps[0] += 1
                if t is None:
                    dve.wait_ge(dve_step, steps[0])
                else:
                    dve.wait_ge(dve_step, t * DVE_TILE + (DVE_BEFORE + steps[0]))

            def rsqrt(out_, sq, n, count, t):
                m, a = rs_m[:, :count], rs_t[:, :count]
                link(V.tensor_scalar(m, sq, 1.0 / n, EPS, ALU.mult, ALU.add), t)
                V.tensor_scalar(out_.bitcast(I32), m.bitcast(I32), -0.5, float(RSQRT_MAGIC), ALU.mult, ALU.add)
                link(V.tensor_scalar(a, m, -0.5, None, ALU.mult), t)
                for _ in range(3):
                    if count == 1:
                        link(V.scalar_tensor_tensor(m, out_, a, out_, ALU.mult, ALU.mult), t)
                    else:
                        link(V.tensor_tensor(m, out_, out_, ALU.mult), t)
                        link(V.tensor_tensor(m, m, a, ALU.mult), t)
                    link(V.scalar_tensor_tensor(out_, m, 1.5, out_, ALU.add, ALU.mult), t)

            def x_scale(T, t):
                dve.wait_ge(x_squared, T + 1)
                rsqrt(rs_x, ssq_x, D, TB, t)
                for i in range(TB):
                    last = V.tensor_scalar(xn[:, i, :], xn[:, i, :], rs_x[:, i:i + 1], None, ALU.mult)
                last.then_inc(x_scaled, 1)

            def affine(T, k, bank, buf):
                dve.wait_ge(xT_full, T * KB_D + (k + 1))
                V.tensor_scalar(buf, bank, gscale[:, k:k + 1], shift[:, k:k + 1], ALU.mult, ALU.add
                                ).then_inc(xT_read[0], 1)

            def h_low(T, k, buf):
                dve.wait_ge(h_hi_ready, T * KB_D + (k + 1))
                V.tensor_tensor(h_lo[:, k, :], buf, h_hi[:, k, :].bitcast(F32), ALU.subtract).then_inc(h_ready, 1)

            V.memset(kT[:, 0:CHUNK], 0.0)
            V.memset(vT[:, 0:CHUNK], 0.0)
            V.memset(state[:, 3, :], 0.0)
            V.memset(ones, 1.0)
            V.memset(zaT[:], 1.0)
            dve.wait_ge(c_tanh_done, 1)
            link(V.scalar_tensor_tensor(c_silu, c_tanh, 1.0, c_col, ALU.add, ALU.mult))
            V.tensor_scalar(c_silu, c_silu, 0.5, None, ALU.mult).then_inc(silu_ready, 1)
            dve.wait_ge(silu_ready, 1)

            def to_columns(row, buf, out_):
                row3, buf3 = (r.rearrange("p (k n) -> p k n", n=P) for r in (row, buf))
                link(V.tensor_tensor(buf3, row3, ident[:].unsqueeze(1).to_broadcast([P, 4, P]), ALU.mult))
                return V.tensor_reduce(out=out_, in_=buf3, op=ALU.add, axis=AX.X)

            def finish_scale(n, buf):
                four = slice(4 * n, 4 * n + 4)
                dve.wait_ge(scale_full, n + 1)
                link(to_columns(mod_banks[1 + n][0], buf, gscale[:, four]))
                link(V.tensor_tensor(gscale[:, four], gscale[:, four], modb[:, 8 + 4 * n:12 + 4 * n], ALU.add))
                V.scalar_tensor_tensor(gscale[:, four], gscale[:, four], 1.0, norm_col[:, four], ALU.add, ALU.mult
                                       ).then_inc(gscale_ready, 1)
                dve.wait_ge(gscale_ready, n + 1)
                dve.sem_inc(acc_free[n], 1)

            x_scale(0, None)

            def weigh(parts, loaded):
                total = parts[0]
                for k, part in enumerate(parts):
                    dve.wait_ge(loaded[k], 16)
                    if k == 0:
                        last = V.tensor_scalar(total, part, c_silu[:, 0:1], None, ALU.mult)
                    else:
                        last = V.scalar_tensor_tensor(total, part, c_silu[:, k:k + 1], total, ALU.mult, ALU.add)
                    if k < len(parts) - 1:
                        link(last)
                return last

            def weigh_group(n):
                weigh([ada_ss[k][:, MOD_GROUPS[n][0]:MOD_GROUPS[n][1]] for k in range(DVE_BLOCKS)], ss_loaded[n]
                      ).then_inc(ss_summed, 1)

            weigh_group(0)
            weigh_group(1)
            dve.wait_ge(ident_loaded, 16)
            dve.wait_ge(shift_full, 1)
            for n in range(2):
                link(to_columns(mod_banks[0][n], h_plain[2 + n], shift[:, 4 * n:4 * n + 4]))
            dve.wait_ge(consts_loaded, 16 * CONSTS)
            link(V.tensor_copy(suffix_r[:], suffix))
            V.tensor_tensor(shift, shift, modb[:, 0:8], ALU.add).then_inc(shift_ready, 1)
            link(V.tensor_scalar(sink8, sink8, SINK_SCALE, None, ALU.mult))
            link(V.tensor_scalar(half_g, half_g, 0.5, None, ALU.mult))
            weigh_group(2)
            finish_scale(0, h_plain[2])
            affine(0, 0, first_banks[0], h_plain[0])
            affine(0, 2, first_banks[2], h_plain[2])
            h_low(0, 0, h_plain[0])
            h_low(0, 1, h_plain[1])
            dve.wait_ge(h_ready, 1)
            finish_scale(1, h_plain[0])
            affine(0, 4, first_banks[4], h_plain[0])
            h_low(0, 2, h_plain[2])
            h_low(0, 3, h_plain[3])
            dve.wait_ge(h_ready, 3)
            affine(0, 6, first_banks[6], h_plain[2])
            for k in range(4, KB_D):
                h_low(0, k, h_plain[k % 4])
            weigh([a[:] for a in ada_gt], gt_loaded).then_inc(gt_summed, 1)
            dve.wait_ge(rows_loaded, 32)
            dve.wait_ge(gate_full, 1)
            V.tensor_tensor(gate_row[:], gate_row[:], ps_s[:].rearrange("p a n -> p (a n)"), ALU.add
                            ).then_inc(gate_ready, 1)
            dve.wait_ge(gate_ready, 1)
            link(V.tensor_scalar(gate_row[:], gate_row[:], 0.5, None, ALU.mult))
            assert steps[0] == DVE_BEFORE, steps
            steps[0] = 0

            with dve.Fori(0, TILES) as t:
                def freed(f):
                    dve.wait_ge(acc_free[f % 2], may_fill(t, f) + 1)

                def gate(f, b, out_):
                    dve.wait_ge(gate_tanh, t * 8 + (b + 1))
                    V.scalar_tensor_tensor(out_, tmp[:, b % 2, :], 1.0, acc[f % 2][:], ALU.add, ALU.mult
                                           ).then_inc(acc_free[f % 2], 1)

                def bias_and_max(u):
                    pair, g, b = u // 2, u % 2, u % 2
                    dve.wait_ge(scores_full, t * 8 + (u + 1))
                    for j in range(A_GROUP):
                        slope = 2.0 ** -(A_GROUP * g + j + 1)
                        last = V.scalar_tensor_tensor(probs[:, b, j, :], dist[:, 1 if pair else 0, :],
                                                      -SINK_SCALE * slope, ps_s[:, j, 0:WIN], ALU.mult, ALU.add)
                    last.then_inc(scores_read, 1)
                    dve.wait_ge(scores_read, t * 8 + (u + 1))
                    link(V.tensor_reduce(out=maxs[:, u, :], in_=probs[:, b, :, :], op=ALU.max, axis=AX.X), t)
                    link(V.tensor_tensor(maxs[:, u, :], maxs[:, u, :], sink8[:, 4 * g:4 * g + 4], ALU.max), t)
                    V.tensor_tensor(esink[:, u, :], sink8[:, 4 * g:4 * g + 4], maxs[:, u, :], ALU.subtract)
                    V.tensor_scalar(nmax[:, u, :], maxs[:, u, :], -1.0 / SINK_SCALE, None, ALU.mult).then_inc(negmax, 1)

                def denominators(u):
                    dve.wait_ge(probs_ready, t * 8 + (u + 1))
                    link(V.tensor_tensor(sums[:, u, :], sums[:, u, :], esink[:, u, :], ALU.add), t)
                    link(V.reciprocal(rden[:, u, :], sums[:, u, :]), t)

                def scale_and_gate(u):
                    pair, g = u // 2, u % 2
                    if g == 0:
                        freed(first_fill(4 * P_GA + pair))
                    dve.wait_ge(pv_full, t * 8 + (u + 1))
                    for j in range(A_GROUP):
                        cols = slice((A_GROUP * g + j) * A_DIM, (A_GROUP * g + j + 1) * A_DIM)
                        last = V.scalar_tensor_tensor(ya[:, pair, cols], ps_y[:, j * A_DIM:(j + 1) * A_DIM],
                                                      rden[:, u, j:j + 1], ya[:, pair, cols], ALU.mult, ALU.mult)
                    last.then_inc(y_scaled, 1)

                def y_low(n):
                    dve.wait_ge(yT_hi_ready, t * 8 + (n + 1))
                    V.scalar_tensor_tensor(y_lo[:, n, :], ps_t[:, n % 2, :], 0.5 if n < 4 else half_g,
                                           y_hi[:, n, :].bitcast(F32), ALU.mult, ALU.subtract).then_inc(yT_ready, 1)

                def update_state(i):
                    dve.wait_ge(kv_full, t * 4 + (i + 1))
                    for c2 in range(2):
                        ch = 2 * i + c2
                        for hp in range(2):
                            cols = slice(hp * P, (hp + 1) * P)
                            last = V.scalar_tensor_tensor(state[:, ch % 4, cols], state[:, (ch - 1) % 4, cols],
                                                          decay[:, hp * 8 + ch:hp * 8 + ch + 1],
                                                          ps_s[:, 2 * c2, cols],
                                                          ALU.mult, ALU.add)
                        if c2 == 0:
                            link(last, t)
                    last.then_inc(state_ready, 1)
                    dve.wait_ge(state_ready, t * 4 + (i + 1))

                def final_rsqrt(i):
                    dve.wait_ge(res_squared, t * 4 + (i + 1))
                    rsqrt(rs_f[:, i:i + 1], ssq_f[:, i:i + 1], D, 1, t)

                def final_scale(i):
                    V.scalar_tensor_tensor(res[:, i, :], res[:, i, :], rs_f[:, i:i + 1], final_row[:],
                                           ALU.mult, ALU.mult).then_inc(result_ready, 1)

                def merge(s, q, j):
                    f, n = first_fill(s), 4 * q + j
                    if j == 0:
                        freed(first_fill(4 * P_ZM[2 * q + 1] + 2))
                        freed(first_fill(4 * P_ZM[2 * q + 1] + 3))
                    if n >= 2:
                        dve.wait_ge(m_ready, t * 8 + (n - 1))
                    dve.wait_ge(acc_full, filled(t, f))
                    V.scalar_tensor_tensor(tmp[:, j % 2, :], gate_a[:, j, :], 1.0, acc[f % 2][:], ALU.add, ALU.mult
                                           ).then_inc(acc_free[f % 2], 1)
                    dve.wait_ge(acc_full, filled(t, f + 1))
                    V.scalar_tensor_tensor(tmp2[:, j % 2, :], gate_b[:, j, :], 1.0, acc[(f + 1) % 2][:], ALU.add, ALU.mult
                                           ).then_inc(acc_free[(f + 1) % 2], 1)
                    freed(f)
                    freed(f + 1)
                    V.tensor_tensor(tmp[:, j % 2, :], tmp[:, j % 2, :], tmp2[:, j % 2, :], ALU.add).then_inc(m_plain, 1)
                    dve.wait_ge(m_hi_ready, t * 8 + (n + 1))
                    V.tensor_tensor(m_lo[:, n, :], tmp[:, j % 2, :], m_hi[:, n, :].bitcast(F32), ALU.subtract
                                    ).then_inc(m_ready, 1)

                for s in range(SLOTS):
                    panel, b = s // 4, s % 4
                    f = first_fill(s)
                    a = acc[f % 2]
                    if panel == P_KVQ and b < 2 or panel == P_KZ:
                        dve.wait_ge(acc_full, filled(t, f))
                    if panel == P_KVQ and b == 0:
                        V.tensor_copy(kT[:, CHUNK:], a[:]).then_inc(acc_free[f % 2], 1)
                    if panel == P_KVQ and b == 1:
                        V.tensor_copy(vT[:, CHUNK:], a[:]).then_inc(acc_free[f % 2], 1)
                    if panel == P_KZ:
                        V.tensor_copy(kb[:, b, :], a[:, 0:256])
                        V.tensor_copy(za[:, b, :], a[:, 256:256 + RANK]).then_inc(acc_free[f % 2], 1)
                    if panel == P_GA:
                        gate(f, b, ya[:, b, :])
                    if panel == P_GB:
                        gate(f, 4 + b, yb[:, b, :])
                    if s == 6:
                        dve.wait_ge(stored, t * (16 * TB) + 16)
                        dve.wait_ge(vT_full, t + 1)
                        V.tensor_copy(v_win[:].rearrange("p w i c -> p (w i c)"), ps_t[:].rearrange("p w n -> p (w n)")
                                      ).then_inc(v_ready, 1)
                    if 0 <= s - 7 < 8:
                        bias_and_max(s - 7)
                    if 0 <= s - 9 < 8:
                        scale_and_gate(s - 9)
                    if 0 <= s - 8 < 8:
                        denominators(s - 8)
                    if s == 16:
                        dve.wait_ge(zaT_full, t + 1)
                        V.tensor_copy(zaT[0:RANK, :], ps_t[0:RANK, 0, :]).then_inc(zaT_ready, 1)
                    if s == 18:
                        dve.wait_ge(log_ready, t + 1)
                        V.scalar_tensor_tensor(la[:], ps_s[:], 0.0, lscr[:], ALU.min, ALU.subtract).then_inc(la_ready, 1)
                        V.tensor_copy(kT[:, 0:CHUNK], kT[:, NT:NT + CHUNK])
                        V.tensor_copy(vT[:, 0:CHUNK], vT[:, NT:NT + CHUNK])
                        link(V.tensor_copy(dist[:, 0, :], dist[:, 1, :]), t)
                        dve.wait_ge(la_hi_ready, t + 1)
                        V.tensor_tensor(la_lo[:], la[:], la_hi[:].bitcast(F32), ALU.subtract).then_inc(la_split, 1)
                    if s == 19:
                        dve.wait_ge(decay_ready, t + 1)
                        V.tensor_tensor(kb[:], kb[:], lscr[:], ALU.mult).then_inc(kb_ready, 1)
                    if 20 <= s < 24:
                        update_state(s - 20)
                        y_low(s - 20)
                    if 21 <= s < 25:
                        i = s - 21
                        freed(first_fill(4 * P_GB + i))
                        dve.wait_ge(o_squared, t * 4 + (i + 1))
                        for low, o in enumerate((ps_o, ps_y)):
                            heads = yb[:, i, :].rearrange("p (h l e) -> p l h e", l=2, e=B_V)[:, low]
                            last = V.tensor_tensor(heads, heads, o[:, 0:256].rearrange("p (h e) -> p h e", e=B_V), ALU.mult)
                        last.then_inc(o_gated, 1)
                    if s == 25:
                        dve.wait_ge(o_squared, t * 4 + 4)
                        rsqrt(rs_o, ssq_o, B_V, 4 * TB, t)
                        dve.wait_ge(o_gated, t * 4 + 4)
                        yb3 = yb[:].rearrange("p i (h e) -> p (i h) e", e=B_V)
                        V.tensor_tensor(yb3, yb3, rs_o.unsqueeze(2).to_broadcast([P, 4 * TB, B_V]), ALU.mult
                                        ).then_inc(yb_ready, 1)
                    if 27 <= s < 31:
                        y_low(s - 23)
                    if panel in P_BR:
                        merge(s, P_BR.index(panel), b)
                    if s == 50:
                        x_scale(t + 1, t)
                    if s >= 53:
                        final_rsqrt(s - 53)
                    if panel in P_OUT:
                        cols = slice(P_OUT.index(panel) * 512, P_OUT.index(panel) * 512 + 512)
                        if panel == P_OUT[0]:
                            dve.wait_ge(res_loaded[b], t * 16 + 16)
                        n = 4 * P_OUT.index(panel) + b
                        if n >= 2:
                            dve.wait_ge(res_ready, t * 8 + (n - 1))
                        dve.wait_ge(acc_full, filled(t, f))
                        V.tensor_tensor(tmp[:, b % 2, :], a[:], gate_row[:, cols], ALU.mult).then_inc(acc_free[f % 2], 1)
                        freed(f)
                        V.tensor_tensor(res[:, b, cols], res[:, b, cols], tmp[:, b % 2, :], ALU.add).then_inc(res_ready, 1)
                    if 51 <= s < 55:
                        k = 2 * (s - 51)
                        if k:
                            dve.wait_ge(h_ready, (t + 1) * KB_D + (k - 1))
                        affine(t + 1, k, ps_t[:, 0, :], h_plain[0])
                        h_low(t + 1, k, h_plain[0])
                        h_low(t + 1, k + 1, h_plain[1])
                    if s >= 53:
                        final_scale(s - 53)
                    if s == 55:
                        final_rsqrt(3)
                        final_scale(3)
                assert steps[0] == DVE_TILE, steps

        @block.scalar
        def _(act):
            A = nc.scalar.activation
            steps = [0]
            ACT_BEFORE, ACT_TILE = 3, 5

            def link(ins, t=None):
                ins.then_inc(act_step, 1)
                steps[0] += 1
                if t is None:
                    act.wait_ge(act_step, steps[0])
                else:
                    act.wait_ge(act_step, t * ACT_TILE + (ACT_BEFORE + steps[0]))

            act.sem_inc(stored, 16)
            act.wait_ge(c_loaded, 16)
            A(c_tanh, c_col, ACT.Tanh, scale=0.5).then_inc(c_tanh_done, 1)
            for dst, src in ((modb, ada_b), (norm_col, norm_g), (half_g, head_g),
                             (sink8, sinks.partition_broadcast(P)),
                             (suffix, suffix_in), (chunks[:], chunks_in), (dist[:], dist_in)):
                act.dma_start(dst, src).then_inc(consts_loaded, 16)
            act.dma_start(w_al[0:RANK, :], w_alpha).then_inc(consts_loaded, 16)
            act.dma_start(w_al[RANK:RANK + 1, :], b_alpha).then_inc(consts_loaded, 16)

            def x_square(T, t, blocks=(0, 1, 2, 3)):
                junk = squares[:] if t is not None else tmp2[:].rearrange("p a n -> p (a n)")
                for i in blocks:
                    act.wait_ge(x_loaded[i], 16 * T + 16)
                    square = A(junk, xn[:, i, :], ACT.Square, accum_out=ssq_x[:, i:i + 1])
                    if i == 3:
                        square.then_inc(x_squared, 1)
                    else:
                        link(square, t)

            def affine(T, k, bank, buf):
                act.wait_ge(xT_full, T * KB_D + (k + 1))
                A(buf, bank, ACT.Identity, bias=shift[:, k:k + 1], scale=gscale[:, k:k + 1]).then_inc(xT_read[1], 1)

            def h_high(T, k, buf):
                act.wait_ge(xT_read[k % 2], T * 4 + (k // 2 + 1))
                A(h_hi[:, k, :], buf, ACT.Copy).then_inc(h_hi_ready, 1)

            x_square(0, None)
            for k in range(0, KB_D, 2):
                act.wait_ge(gscale_ready, 1 + (k + 1) // 4)
                if k >= 4:
                    act.wait_ge(h_ready, k - 2)
                affine(0, k + 1, first_banks[k + 1], h_plain[(k + 1) % 4])
                h_high(0, k, h_plain[k % 4])
                h_high(0, k + 1, h_plain[(k + 1) % 4])
                for kk in (k, k + 1):
                    act.dma_start(ada_gt[kk][:], ada_w[kk * P:(kk + 1) * P, 2 * D:3 * D]).then_inc(gt_loaded[kk], 16)
            act.dma_start(gate_row[:], ada_b_row.partition_broadcast(P)).then_inc(rows_loaded, 16)
            act.dma_start(final_row[:], final_g.partition_broadcast(P)).then_inc(rows_loaded, 16)

            assert steps[0] == ACT_BEFORE, steps
            steps[0] = 0

            with act.Fori(0, TILES) as t:
                def store(i):
                    act.wait_ge(result_ready, t * 4 + (i + 1))
                    act.dma_start(out[bass.ds(t * NT + i * P, P), :], res[:, i, :]).then_inc(stored, 16)

                for s in range(SLOTS):
                    panel, b = s // 4, s % 4
                    f = first_fill(s)
                    a = acc[f % 2]
                    if panel in (P_QA, P_VB, P_GA, P_GB) + P_ZM or panel == P_KVQ and b >= 2:
                        act.wait_ge(acc_full, filled(t, f))
                    if panel == P_QA:
                        A(qT[:, b, :], a[:], ACT.Copy).then_inc(acc_free[f % 2], 1)
                    if panel == P_KVQ and b >= 2:
                        A(qbT[:, b - 2, :], a[:], ACT.Copy, scale=B_K ** -0.5).then_inc(acc_free[f % 2], 1)
                    if panel == P_VB:
                        A(vb[:, b, :], a[:], ACT.Copy).then_inc(acc_free[f % 2], 1)
                    if panel in (P_GA, P_GB):
                        A(tmp[:, b % 2, :], a[:], ACT.Tanh, scale=0.5).then_inc(gate_tanh, 1)
                    if panel in P_ZM:
                        dst = (gate_a, gate_b)[P_ZM.index(panel) % 2]
                        A(dst[:, b, :], a[:], ACT.Tanh, scale=0.5).then_inc(acc_free[f % 2], 1)
                    if 0 <= s - 8 < 8:
                        u = s - 8
                        act.wait_ge(ptrans_full, t * 8 + (u + 1))
                        A(probsT[:, u % 2, :, :].rearrange("p j q -> p (j q)"), ps_t[:, u % 2, :], ACT.Copy
                          ).then_inc(ptrans_read, 1)
                    if 0 <= s - 7 < 8:
                        u = s - 7
                        act.wait_ge(negmax, t * 8 + (u + 1))
                        for j in range(A_GROUP):
                            pr = probs[:, u % 2, j, :]
                            A(pr, pr, ACT.Exp, bias=nmax[:, u, j:j + 1], scale=1.0 / SINK_SCALE,
                              accum_out=sums[:, u, j:j + 1])
                        A(esink[:, u, :], esink[:, u, :], ACT.Exp, scale=1.0 / SINK_SCALE).then_inc(probs_ready, 1)
                    if s == 17:
                        act.wait_ge(z_full, t + 1)
                        link(A(lscr[:], ps_s[:], ACT.Abs), t)
                        link(A(lscr[:], lscr[:], ACT.Exp, scale=-1.0), t)
                        A(lscr[:], lscr[:], ACT.Ln, bias=1.0).then_inc(log_ready, 1)
                    if s == 18:
                        act.wait_ge(la_ready, t + 1)
                        A(la_hi[:], la[:], ACT.Copy).then_inc(la_hi_ready, 1)
                    if s == 19:
                        act.wait_ge(cum_full, t + 1)
                        A(lscr[:], ps_s[:], ACT.Exp)
                        A(decay, ps_y[:, 0:16], ACT.Exp).then_inc(decay_ready, 1)
                    if 21 <= s < 25:
                        i = s - 21
                        if i:
                            act.wait_ge(o_squared, t * 4 + i)
                        act.wait_ge(o_full, t * 4 + (i + 1))
                        for hd in range(B_HEADS):
                            hp, low = hd // 2, hd % 2
                            last = A(tmp2[:, 0, hd * B_V:(hd + 1) * B_V],
                                     (ps_o, ps_y)[low][:, hp * B_V:(hp + 1) * B_V], ACT.Square,
                                     accum_out=ssq_o[:, i * 4 + hd:i * 4 + hd + 1])
                        last.then_inc(o_squared, 1)
                    if 20 <= s < 24 or 27 <= s < 31:
                        n = s - 20 if s < 24 else s - 23
                        act.wait_ge(yT_full, t * 8 + (n + 1))
                        A(y_hi[:, n, :], ps_t[:, n % 2, :], ACT.Identity, scale=0.5 if n < 4 else half_g
                          ).then_inc(yT_hi_ready, 1)
                    if panel in P_BR:
                        n = 4 * P_BR.index(panel) + b
                        act.wait_ge(m_plain, t * 8 + (n + 1))
                        A(m_hi[:, n, :], tmp[:, b % 2, :], ACT.Copy).then_inc(m_hi_ready, 1)
                    if s == 4 * P_BR[1] + 2:
                        act.wait_ge(m_ready, t * 8 + 6)
                        for i in (0, 2):
                            act.dma_start(xn[:, i, :], x_block((t + 1) % TILES, i)).then_inc(x_loaded[i], 16)
                    if s == 4 * P_BR[1] + 3:
                        act.wait_ge(m_ready, t * 8 + 8)
                        act.dma_start(res[:, 0, :], x_block(t, 0)).then_inc(res_loaded[0], 16)
                        for i in (1, 3):
                            act.dma_start(xn[:, i, :], x_block((t + 1) % TILES, i)).then_inc(x_loaded[i], 16)
                        for i in (1, 2, 3):
                            act.dma_start(res[:, i, :], x_block(t, i)).then_inc(res_loaded[i], 16)
                    if s == 48:
                        x_square(t + 1, t, (0, 2))
                    if s == 49:
                        x_square(t + 1, t, (1, 3))
                    if 51 <= s < 55:
                        k = 2 * (s - 51)
                        if k:
                            act.wait_ge(h_ready, (t + 1) * KB_D + k)
                        affine(t + 1, k + 1, ps_t[:, 1, :], h_plain[1])
                        h_high(t + 1, k, h_plain[0])
                        h_high(t + 1, k + 1, h_plain[1])
                    if s >= 52:
                        i = s - 52
                        if i == 0:
                            act.wait_ge(x_squared, t + 2)
                        else:
                            act.wait_ge(res_squared, t * 4 + i)
                        act.wait_ge(res_ready, t * 8 + (5 + i))
                        A(squares[:], res[:, i, :], ACT.Square, accum_out=ssq_f[:, i:i + 1]).then_inc(res_squared, 1)
                        if s >= 54:
                            store(s - 54)
                assert steps[0] == ACT_TILE, steps
                store(2)
                store(3)


def shape_constants():
    r = np.arange(P)
    ident = np.eye(P, dtype=np.float32)
    same = r[:, None] // CHUNK == r[None, :] // CHUNK
    suffix = (same & (r[:, None] > r[None, :])).astype(np.float32) / np.float32(16.0)
    chunks = (r[:, None] // CHUNK == np.arange(2)[None, :]).astype(np.float32) / np.float32(16.0)
    inner = np.abs(CHUNK + r[:, None] % CHUNK - np.arange(WIN)[None, :]).astype(np.float32)
    missing = (r[:, None] < CHUNK) & (np.arange(WIN)[None, :] < CHUNK)
    first = np.where(missing, np.float32(MASKED), inner)
    dist = np.ascontiguousarray(np.stack([first, inner], axis=1).astype(np.float32))
    return ident, suffix, chunks, dist


def kernel(x, c, ada_w, ada_b, norm_g, w_in, w_alpha, b_alpha, sinks, head_norm_g,
           w_branch_a, w_branch_b, w_out, final_norm_g):
    from concourse import bacc
    from concourse.bass_utils import run_bass_kernel_spmd

    def columns(a):
        return np.ascontiguousarray(np.asarray(a).reshape(-1, P).T)

    a = {k: np.asarray(v) for k, v in dict(
        x=x, c=c, ada_w=ada_w, ada_b=ada_b, norm_g=norm_g, w_in=w_in, w_alpha=w_alpha, b_alpha=b_alpha, sinks=sinks,
        head_norm_g=head_norm_g, w_branch_a=w_branch_a, w_branch_b=w_branch_b, w_out=w_out,
        final_norm_g=final_norm_g).items()}
    ident, suffix, chunks, dist = shape_constants()
    inputs = [
        ("x", a["x"][0]), ("c", columns(a["c"][0])), ("ada_w", a["ada_w"][0]), ("ada_b", columns(a["ada_b"][0, :2 * D])),
        ("norm_g", columns(a["norm_g"][0])), ("w_in", a["w_in"][0]), ("w_alpha", a["w_alpha"][0]),
        ("b_alpha", a["b_alpha"]), ("sinks", a["sinks"][0]), ("head_g", columns(a["head_norm_g"][0])),
        ("w_br_a", a["w_branch_a"][0]), ("w_br_b", a["w_branch_b"][0]), ("w_out", a["w_out"][0]),
        ("final_g", a["final_norm_g"]), ("ada_b_row", a["ada_b"][0, 2 * D:]),
        ("ident", ident), ("suffix", suffix), ("chunks", chunks), ("dist", dist),
    ]
    nc = bacc.Bacc("TRN2", target_bir_lowering=False, num_devices=1)
    arrays, args = {}, []
    for name, value in inputs:
        value = np.ascontiguousarray(value)
        arrays["in_" + name] = value
        args.append(nc.dram_tensor("in_" + name, value.shape, mybir.dt.from_np(value.dtype), kind="ExternalInput").ap())
    out = nc.dram_tensor("out_0", (SEQ, D), mybir.dt.float32, kind="ExternalOutput").ap()
    build(nc, *args, out)
    r = run_bass_kernel_spmd(nc, [arrays], core_ids=[0])
    return np.asarray(r.results[0]["out_0"]).reshape(1, SEQ, D)
```
